# Optimizing a Trainium2 kernel written in Bass

```python
import jax, jax.numpy as jnp
from jax import lax
import numpy as np
import math

D_MODEL = 2048
BATCH = 1
SEQ = 256
DEPTH = 1

GMLP_WIDTH = 1024
GMLP_GROUPS = 8
GMLP_GROUP_DIM = GMLP_WIDTH // GMLP_GROUPS
CHUNK = 128
ATTN_HEADS = 8
HEAD_DIM = 128
ATTN_WIDTH = ATTN_HEADS * HEAD_DIM
Q_LORA_RANK = 512
IDX_HEADS = 16
IDX_HEAD_DIM = 64
IDX_ROPE_DIM = 32
INDEX_TOPK = 256
QUERY_BLOCK = 128
ROPE_THETA = 10000.0
FFN_HIDDEN = -(-8 * D_MODEL // (3 * 256)) * 256
N_MOD = 6
NORM_EPS = 1e-6

COL_UV = 0
COL_QLAT = COL_UV + 2 * GMLP_WIDTH
COL_K = COL_QLAT + Q_LORA_RANK
COL_V = COL_K + ATTN_WIDTH
COL_KIDX = COL_V + ATTN_WIDTH
COL_IDXW = COL_KIDX + IDX_HEAD_DIM
COL_GATE = COL_IDXW + IDX_HEADS
IN_COLS = COL_GATE + 2 * D_MODEL


def rms_norm(x, g):
    xf = x.astype(jnp.float32)
    y = xf * lax.rsqrt(jnp.mean(xf * xf, axis=-1, keepdims=True) + NORM_EPS)
    return (y * g.astype(jnp.float32)).astype(x.dtype)

def layer_norm(x, g, b):
    xf = x.astype(jnp.float32)
    mu = jnp.mean(xf, axis=-1, keepdims=True)
    xc = xf - mu
    var = jnp.mean(xc * xc, axis=-1, keepdims=True)
    return (xc * lax.rsqrt(var + NORM_EPS) * g.astype(jnp.float32) + b.astype(jnp.float32)).astype(x.dtype)

def rope_tables(seq, dim):
    inv = 1.0 / (ROPE_THETA ** (jnp.arange(0, dim, 2, dtype=jnp.float32) / dim))
    ang = jnp.arange(seq, dtype=jnp.float32)[:, None] * inv[None, :]
    return jnp.cos(ang), jnp.sin(ang)

def apply_rope(x, cos, sin):
    xf = x.astype(jnp.float32)
    half = xf.shape[-1] // 2
    x1, x2 = xf[..., :half], xf[..., half:]
    c = cos[None, :, None, :]
    s = sin[None, :, None, :]
    return jnp.concatenate([x1 * c - x2 * s, x2 * c + x1 * s], axis=-1).astype(x.dtype)

def apply_partial_rope(x, cos, sin):
    return jnp.concatenate([apply_rope(x[..., :IDX_ROPE_DIM], cos, sin), x[..., IDX_ROPE_DIM:]], axis=-1)

def gmlp_spatial_gating(uv, ln_g, ln_b, w_s, b_s):
    B, S, _ = uv.shape
    z = jax.nn.gelu(uv)
    u, v = z[..., :GMLP_WIDTH], z[..., GMLP_WIDTH:]
    v = layer_norm(v, ln_g, ln_b)
    v = v.reshape(B, S // CHUNK, CHUNK, GMLP_GROUPS, GMLP_GROUP_DIM)
    causal = jnp.tril(jnp.ones((CHUNK, CHUNK), dtype=bool))
    w = jnp.where(causal[None], w_s, 0).astype(v.dtype)
    sv = jnp.einsum('gts,bcsgd->bctgd', w, v) + b_s.T.astype(v.dtype)[None, None, :, :, None]
    return u * sv.reshape(B, S, GMLP_WIDTH)

def dsa_attention(q, k, v, q_idx, k_idx, idx_w):
    B, S, H, Dh = q.shape
    topk = min(INDEX_TOPK, S // 4)
    n_blocks = S // QUERY_BLOCK
    key_pos = jnp.arange(S)
    scale = HEAD_DIM ** -0.5
    gather = jax.vmap(lambda kk, ii: kk[ii])

    def one_block(i):
        t0 = i * QUERY_BLOCK
        qb = lax.dynamic_slice_in_dim(q, t0, QUERY_BLOCK, axis=1)
        qib = lax.dynamic_slice_in_dim(q_idx, t0, QUERY_BLOCK, axis=1)
        wb = lax.dynamic_slice_in_dim(idx_w, t0, QUERY_BLOCK, axis=1)
        q_pos = t0 + jnp.arange(QUERY_BLOCK)
        causal = key_pos[None, :] <= q_pos[:, None]
        logits = jnp.einsum('bqhd,bsd->bqhs', qib, k_idx).astype(jnp.float32)
        score = jnp.einsum('bqhs,bqh->bqs', jax.nn.relu(logits), wb.astype(jnp.float32))
        score = jnp.where(causal[None], score, -jnp.inf)
        _, sel = lax.top_k(score, topk)
        valid = sel <= q_pos[None, :, None]
        k_sel = gather(k, sel)
        v_sel = gather(v, sel)
        att = jnp.einsum('bqhd,bqkhd->bhqk', qb, k_sel).astype(jnp.float32) * scale
        att = jnp.where(valid[:, None], att, -jnp.inf)
        p = jax.nn.softmax(att, axis=-1).astype(v.dtype)
        return jnp.einsum('bhqk,bqkhd->bqhd', p, v_sel)

    out = lax.map(one_block, jnp.arange(n_blocks))
    return out.transpose(1, 0, 2, 3, 4).reshape(B, S, H * Dh)

def first_inputs(seed: int = 0) -> dict:
    key = jax.random.key(seed)
    ks = iter(jax.random.split(key, 32))
    f32 = jnp.float32

    def nrm(shape, scale):
        return jax.random.normal(next(ks), shape, f32) * scale

    def gain(shape):
        return 1.0 + 0.1 * jax.random.normal(next(ks), shape, f32)

    L = DEPTH
    return {
        "x": nrm((BATCH, SEQ, D_MODEL), 1.0),
        "c": nrm((BATCH, D_MODEL), 1.0),
        "w_mod": nrm((L, D_MODEL, N_MOD * D_MODEL), 0.5 * D_MODEL ** -0.5),
        "b_mod": nrm((L, N_MOD * D_MODEL), 0.01),
        "g_pre_mix": gain((L, D_MODEL)),
        "g_post_mix": gain((L, D_MODEL)),
        "w_in": nrm((L, D_MODEL, IN_COLS), D_MODEL ** -0.5),
        "gmlp_ln_g": gain((L, GMLP_WIDTH)),
        "gmlp_ln_b": nrm((L, GMLP_WIDTH), 0.02),
        "gmlp_w_s": nrm((L, GMLP_GROUPS, CHUNK, CHUNK), CHUNK ** -0.5),
        "gmlp_b_s": gain((L, GMLP_GROUPS, CHUNK)),
        "q_lat_norm_g": gain((L, Q_LORA_RANK)),
        "w_q_up": nrm((L, Q_LORA_RANK, ATTN_WIDTH), Q_LORA_RANK ** -0.5),
        "w_qidx_up": nrm((L, Q_LORA_RANK, IDX_HEADS * IDX_HEAD_DIM), Q_LORA_RANK ** -0.5),
        "kidx_ln_g": gain((L, IDX_HEAD_DIM)),
        "kidx_ln_b": nrm((L, IDX_HEAD_DIM), 0.02),
        "w_proj_a": nrm((L, GMLP_WIDTH, D_MODEL), GMLP_WIDTH ** -0.5),
        "w_proj_b": nrm((L, ATTN_WIDTH, D_MODEL), ATTN_WIDTH ** -0.5),
        "w_out": nrm((L, D_MODEL, D_MODEL), D_MODEL ** -0.5),
        "g_pre_ffn": gain((L, D_MODEL)),
        "g_post_ffn": gain((L, D_MODEL)),
        "w_ffn_gate": nrm((L, D_MODEL, FFN_HIDDEN), D_MODEL ** -0.5),
        "w_ffn_up": nrm((L, D_MODEL, FFN_HIDDEN), D_MODEL ** -0.5),
        "w_ffn_down": nrm((L, FFN_HIDDEN, D_MODEL), FFN_HIDDEN ** -0.5),
    }

def first_block(x, c, w_mod, b_mod, g_pre_mix, g_post_mix, w_in, gmlp_ln_g, gmlp_ln_b, gmlp_w_s, gmlp_b_s,
              q_lat_norm_g, w_q_up, w_qidx_up, kidx_ln_g, kidx_ln_b, w_proj_a, w_proj_b, w_out,
              g_pre_ffn, g_post_ffn, w_ffn_gate, w_ffn_up, w_ffn_down):
    B, S, D = x.shape
    cos_a, sin_a = rope_tables(S, HEAD_DIM)
    cos_i, sin_i = rope_tables(S, IDX_ROPE_DIM)
    idx_w_scale = (IDX_HEADS ** -0.5) * (IDX_HEAD_DIM ** -0.5)

    for l in range(DEPTH):
        mod = (c @ w_mod[l] + b_mod[l]).reshape(B, N_MOD, D)
        shift_m, scale_m, gate_m = mod[:, 0, None], mod[:, 1, None], mod[:, 2, None]
        shift_f, scale_f, gate_f = mod[:, 3, None], mod[:, 4, None], mod[:, 5, None]

        h = rms_norm(x, g_pre_mix[l]) * (1 + scale_m) + shift_m
        proj = h @ w_in[l]

        y_a = gmlp_spatial_gating(proj[..., COL_UV:COL_QLAT], gmlp_ln_g[l], gmlp_ln_b[l],
                                  gmlp_w_s[l], gmlp_b_s[l])

        q_lat = rms_norm(proj[..., COL_QLAT:COL_K], q_lat_norm_g[l])
        q = apply_rope((q_lat @ w_q_up[l]).reshape(B, S, ATTN_HEADS, HEAD_DIM), cos_a, sin_a)
        k = apply_rope(proj[..., COL_K:COL_V].reshape(B, S, ATTN_HEADS, HEAD_DIM), cos_a, sin_a)
        v = proj[..., COL_V:COL_KIDX].reshape(B, S, ATTN_HEADS, HEAD_DIM)
        q_idx = apply_partial_rope((q_lat @ w_qidx_up[l]).reshape(B, S, IDX_HEADS, IDX_HEAD_DIM), cos_i, sin_i)
        k_idx = layer_norm(proj[..., COL_KIDX:COL_IDXW], kidx_ln_g[l], kidx_ln_b[l])
        k_idx = apply_partial_rope(k_idx[:, :, None, :], cos_i, sin_i)[:, :, 0, :]
        idx_w = proj[..., COL_IDXW:COL_GATE] * idx_w_scale
        y_b = dsa_attention(q, k, v, q_idx, k_idx, idx_w)

        gates = jax.nn.sigmoid(proj[..., COL_GATE:])
        merged = gates[..., :D] * (y_a @ w_proj_a[l]) + gates[..., D:] * (y_b @ w_proj_b[l])
        mix_out = merged @ w_out[l]
        x = x + gate_m * rms_norm(mix_out, g_post_mix[l])

        h2 = rms_norm(x, g_pre_ffn[l]) * (1 + scale_f) + shift_f
        f = (jax.nn.silu(h2 @ w_ffn_gate[l]) * (h2 @ w_ffn_up[l])) @ w_ffn_down[l]
        x = x + gate_f * rms_norm(f, g_post_ffn[l])

    return x


DEPTH_2 = 2

N_A_LAYERS = DEPTH_2 // 2
N_B_LAYERS = DEPTH_2 - N_A_LAYERS
RMS_EPS = 1e-6

E_A = D_MODEL
POOL_WINDOWS = (2, 4, 8, 16)
N_POOL_GROUPS = len(POOL_WINDOWS)
POOL_GROUP_DIM = E_A // N_POOL_GROUPS

HEADS_PER_GROUP = D_MODEL // HEAD_DIM
DILATED_PAIRS = ((128, 1), (512, 4), (2048, 16))
N_DIL_GROUPS = len(DILATED_PAIRS)
E_B = HEADS_PER_GROUP * HEAD_DIM
NEG_INF = -1e30


def rmsnorm(x, g):
    xf = x.astype(jnp.float32)
    inv = lax.rsqrt(jnp.mean(xf * xf, axis=-1, keepdims=True) + RMS_EPS)
    return (xf * inv).astype(x.dtype) * g

def rope_tables_2(seq):
    inv_freq = 1.0 / (ROPE_THETA ** (jnp.arange(0, HEAD_DIM, 2, dtype=jnp.float32) / HEAD_DIM))
    ang = jnp.arange(seq, dtype=jnp.float32)[:, None] * inv_freq[None, :]
    return jnp.cos(ang), jnp.sin(ang)

def apply_rope_2(t, cos, sin):
    tf = t.astype(jnp.float32)
    t1, t2 = tf[..., : HEAD_DIM // 2], tf[..., HEAD_DIM // 2:]
    c, s = cos[None, :, None, :], sin[None, :, None, :]
    return jnp.concatenate([t1 * c - t2 * s, t2 * c + t1 * s], axis=-1).astype(t.dtype)

def multiscale_causal_pool(u):
    b, s, _ = u.shape
    u4 = u.reshape(b, s, N_POOL_GROUPS, POOL_GROUP_DIM)
    csum = jnp.cumsum(u4.astype(jnp.float32), axis=1)
    csum = jnp.concatenate([jnp.zeros_like(csum[:, :1]), csum], axis=1)
    win = jnp.asarray(POOL_WINDOWS, dtype=jnp.int32)
    t1 = jnp.arange(1, s + 1, dtype=jnp.int32)[:, None]
    lower = jnp.maximum(t1 - win[None, :], 0)
    c_lo = csum[:, lower, jnp.arange(N_POOL_GROUPS)[None, :], :]
    count = jnp.minimum(t1, win[None, :]).astype(jnp.float32)
    mean = (csum[:, 1:] - c_lo) / count[None, :, :, None]
    return (mean - u4.astype(jnp.float32)).astype(u.dtype)

def dilated_window_attention(q, k, v, window, dilation):
    b, s, h, hd = q.shape
    d = dilation
    nb = window // dilation
    m = s // d
    nblk = -(-m // nb)
    m_pad = nblk * nb

    def residues(t):
        return t.reshape(b, m, d, h, hd).transpose(0, 2, 3, 1, 4)

    qr, kr, vr = residues(q), residues(k), residues(v)
    qb = jnp.pad(qr, ((0, 0), (0, 0), (0, 0), (0, m_pad - m), (0, 0))).reshape(b, d, h, nblk, nb, hd)
    kv_pad = ((0, 0), (0, 0), (0, 0), (nb, m_pad - m), (0, 0))
    kp = jnp.pad(kr, kv_pad).reshape(b, d, h, nblk + 1, nb, hd)
    vp = jnp.pad(vr, kv_pad).reshape(b, d, h, nblk + 1, nb, hd)
    kb = jnp.concatenate([kp[:, :, :, :-1], kp[:, :, :, 1:]], axis=4)
    vb = jnp.concatenate([vp[:, :, :, :-1], vp[:, :, :, 1:]], axis=4)

    scores = jnp.einsum('bdhnqc,bdhnkc->bdhnqk', qb, kb).astype(jnp.float32) * (1.0 / math.sqrt(hd))
    r_idx = jnp.arange(nb)[:, None]
    c_idx = jnp.arange(2 * nb)[None, :]
    band = (c_idx >= r_idx) & (c_idx <= r_idx + nb)
    blk = jnp.arange(nblk)[:, None, None]
    mask = band[None] & (blk * nb + c_idx[None] >= nb)
    scores = jnp.where(mask[None, None, None], scores, NEG_INF)
    lse = jax.nn.logsumexp(scores, axis=-1)
    p = jnp.exp(scores - lse[..., None]).astype(v.dtype)
    out = jnp.einsum('bdhnqk,bdhnkc->bdhnqc', p, vb)

    out = out.reshape(b, d, h, m_pad, hd)[:, :, :, :m]
    lse = lse.reshape(b, d, h, m_pad)[:, :, :, :m]
    out = out.transpose(0, 3, 1, 2, 4).reshape(b, s, h, hd)
    lse = lse.transpose(0, 3, 1, 2).reshape(b, s, h)
    return out, lse

def second_inputs(seed: int = 0) -> dict:
    key = jax.random.key(seed)
    ks = jax.random.split(key, 13)
    f32 = jnp.float32
    x = jax.random.normal(ks[0], (BATCH, SEQ, D_MODEL), f32)
    norm_a = 1.0 + 0.1 * jax.random.normal(ks[1], (N_A_LAYERS, D_MODEL), f32)
    w_in_a = jax.random.normal(ks[2], (N_A_LAYERS, D_MODEL, 2 * E_A), f32) * D_MODEL ** -0.5
    w_grp_a = jax.random.normal(ks[3], (N_A_LAYERS, N_POOL_GROUPS, POOL_GROUP_DIM, POOL_GROUP_DIM), f32) * POOL_GROUP_DIM ** -0.5
    scale_a = 1.0 + 0.1 * jax.random.normal(ks[4], (N_A_LAYERS, E_A), f32)
    w_out_a = jax.random.normal(ks[5], (N_A_LAYERS, E_A, D_MODEL), f32) * E_A ** -0.5
    norm_kv = 1.0 + 0.1 * jax.random.normal(ks[6], (D_MODEL,), f32)
    w_k = jax.random.normal(ks[7], (D_MODEL, E_B), f32) * D_MODEL ** -0.5
    w_v = jax.random.normal(ks[8], (D_MODEL, E_B), f32) * D_MODEL ** -0.5
    norm_b = 1.0 + 0.1 * jax.random.normal(ks[9], (N_B_LAYERS, D_MODEL), f32)
    w_in_b = jax.random.normal(ks[10], (N_B_LAYERS, D_MODEL, N_DIL_GROUPS * E_B + E_B), f32) * D_MODEL ** -0.5
    w_out_b = jax.random.normal(ks[11], (N_B_LAYERS, E_B, D_MODEL), f32) * E_B ** -0.5
    norm_f = 1.0 + 0.1 * jax.random.normal(ks[12], (D_MODEL,), f32)
    return {"x": x, "norm_a": norm_a, "w_in_a": w_in_a, "w_grp_a": w_grp_a, "scale_a": scale_a,
            "w_out_a": w_out_a, "norm_kv": norm_kv, "w_k": w_k, "w_v": w_v, "norm_b": norm_b,
            "w_in_b": w_in_b, "w_out_b": w_out_b, "norm_f": norm_f}

def second_block(x, norm_a, w_in_a, w_grp_a, scale_a, w_out_a, norm_kv, w_k, w_v, norm_b, w_in_b, w_out_b, norm_f):
    b, s, _ = x.shape
    cos, sin = rope_tables_2(s)
    k_shared = None
    v_shared = None
    for layer in range(DEPTH_2):
        if layer < N_A_LAYERS:
            i = layer
            hdn = rmsnorm(x, norm_a[i])
            proj = hdn @ w_in_a[i]
            u, gate = proj[..., :E_A], proj[..., E_A:]
            pooled = multiscale_causal_pool(u)
            y = jnp.einsum('bsgc,gcd->bsgd', pooled, w_grp_a[i]).reshape(b, s, E_A) * scale_a[i]
            x = x + (y * jax.nn.silu(gate)) @ w_out_a[i]
            if layer == N_A_LAYERS - 1:
                kv_in = rmsnorm(x, norm_kv)
                k_shared = apply_rope_2((kv_in @ w_k).reshape(b, s, HEADS_PER_GROUP, HEAD_DIM), cos, sin)
                v_shared = (kv_in @ w_v).reshape(b, s, HEADS_PER_GROUP, HEAD_DIM)
        else:
            i = layer - N_A_LAYERS
            hdn = rmsnorm(x, norm_b[i])
            proj = hdn @ w_in_b[i]
            q_all = proj[..., : N_DIL_GROUPS * E_B].reshape(b, s, N_DIL_GROUPS, HEADS_PER_GROUP, HEAD_DIM)
            gate = proj[..., N_DIL_GROUPS * E_B:]
            outs = []
            lses = []
            for g, (window, dilation) in enumerate(DILATED_PAIRS):
                q = apply_rope_2(q_all[:, :, g], cos, sin)
                o_g, lse_g = dilated_window_attention(q, k_shared, v_shared, window, dilation)
                outs.append(o_g)
                lses.append(lse_g)
            alpha = jax.nn.softmax(jnp.stack(lses, axis=0), axis=0)
            merged = jnp.sum(alpha[..., None].astype(x.dtype) * jnp.stack(outs, axis=0), axis=0)
            merged = merged.reshape(b, s, E_B)
            x = x + (merged * jax.nn.silu(gate)) @ w_out_b[i]
    return rmsnorm(x, norm_f)


def setup_inputs(seed=0):
    out = dict(first_inputs(seed))
    for name, value in second_inputs(seed + 1).items():
        if name != "x":
            out[name + "_2"] = value
    return out


def reference(
    x, c, w_mod, b_mod, g_pre_mix, g_post_mix, w_in, gmlp_ln_g, gmlp_ln_b, gmlp_w_s, gmlp_b_s,
    q_lat_norm_g, w_q_up, w_qidx_up, kidx_ln_g, kidx_ln_b, w_proj_a, w_proj_b, w_out, g_pre_ffn,
    g_post_ffn, w_ffn_gate, w_ffn_up, w_ffn_down, norm_a_2, w_in_a_2, w_grp_a_2, scale_a_2,
    w_out_a_2, norm_kv_2, w_k_2, w_v_2, norm_b_2, w_in_b_2, w_out_b_2, norm_f_2,
):
    x = first_block(
        x, c, w_mod, b_mod, g_pre_mix, g_post_mix, w_in, gmlp_ln_g, gmlp_ln_b, gmlp_w_s,
        gmlp_b_s, q_lat_norm_g, w_q_up, w_qidx_up, kidx_ln_g, kidx_ln_b, w_proj_a, w_proj_b,
        w_out, g_pre_ffn, g_post_ffn, w_ffn_gate, w_ffn_up, w_ffn_down,
    )
    return second_block(
        x, norm_a_2, w_in_a_2, w_grp_a_2, scale_a_2, w_out_a_2, norm_kv_2, w_k_2, w_v_2,
        norm_b_2, w_in_b_2, w_out_b_2, norm_f_2,
    )


_drawn_inputs = setup_inputs


def setup_inputs(seed=0):
    import zlib

    import numpy as np

    out = dict(_drawn_inputs(seed))
    spreads = {}
    factors = {'gmlp_ln_b': 8.0, 'kidx_ln_b': 5.438, 'norm_kv_2': 3.58, 'norm_b_2': 3.432}
    for name, (base, spread) in spreads.items():
        noise = np.random.default_rng([zlib.crc32(name.encode()), seed]).standard_normal(out[name].shape)
        drawn = base * np.exp(spread * noise) if base else spread * noise
        out[name] = __import__('jax').numpy.asarray(drawn.astype(out[name].dtype))
    for name, factor in factors.items():
        out[name] = (out[name] * factor).astype(out[name].dtype)
    return out
```

```python
from contextlib import ExitStack, contextmanager

import numpy as np

import concourse.bass as bass
from concourse import mybir

F32 = mybir.dt.float32
F32R = mybir.dt.float32r
BF16 = mybir.dt.bfloat16
ALU = mybir.AluOpType
ACT = mybir.ActivationFunctionType
AX_X = mybir.AxisListType.X

P = 128
TT = 2
T = TT * P
D = 2048
KD = D // P
N = 512
UNIT = 1024
RING = 4
GW = 1024
HEADS1, HEADS2, HD = 8, 16, 128
QLAT = 512
IH, IDIM, IROPE = 16, 64, 32
TOPK = 64
FFN = 5632
FT = FFN // N
FK = FFN // P
NG = 3
HN = NG * HD
EPS = 1e-6
SCALE = HD ** -0.5
IDX_SCALE = IH ** -0.5 * IDIM ** -0.5
BIG = 1e30
TAKEN = -3e38

START_BLOCKS = 8
LATE_BLOCKS = 16
MOD_UNITS = KD // 2

FM, FM_COLS = {}, 0
for _name, _cols in (("c", KD), ("b_mod", 96), ("g_pre_mix", KD), ("g_post_mix", KD), ("qlat_g", 4),
                     ("g_pre_ffn", KD), ("g_post_ffn", KD), ("norm_a", KD), ("scale_a", KD),
                     ("norm_kv", KD), ("norm_b", KD), ("norm_f", KD), ("b_s", 8)):
    FM[_name] = FM_COLS
    FM_COLS += _cols
GATE_M, SCALE_F, SHIFT_F, GATE_F = (4 * (START_BLOCKS + 4 * i) for i in range(4))

A_UNITS = 8 + 2 + 2 * 8 + 4 + 4 + 2 * 8 + 4 * 8 + 8 * 8 + 4 * 8 + 4 * 8 + FT * 16 + 4 * (FK // 2) + 4 * 20 + 3 * 32
B_UNITS = HEADS2 * 8
C_UNITS = 64
START_UNITS = START_BLOCKS * MOD_UNITS

TILES_BEFORE_MERGE = 10 + 4 + 8
TILES_BEFORE_OUT_A = TILES_BEFORE_MERGE + 8 + 4 + 2 * FT + 4 + 8
TILES_BEFORE_OUT_B = TILES_BEFORE_OUT_A + 4 + 8 + HEADS2 + 4
K_COPIED = KD // 2 + 1 + 2
COPIES_BEFORE_K2 = K_COPIED + 2 + 8 + HEADS1


class Counts:

    def __init__(self):
        self.n, self.turn, self.steps = {}, None, {}

    def at(self, name, div=1):
        n = self.n.get(name, 0) // div
        step = self.steps.get(name, 0)
        if self.turn is None or not step:
            return n
        assert step % div == 0
        return self.turn * (step // div) + n

    def up(self, name, k=1, div=1):
        self.n[name] = self.n.get(name, 0) + k
        return self.at(name, div)

    def slot(self, name, ring):
        assert self.turn is None or self.steps.get(name, 0) % ring == 0, name
        return self.n.get(name, 0) % ring

    @contextmanager
    def loop(self, engine, turns, **steps):
        first = dict(self.n)
        self.steps = steps
        with engine.Fori(0, turns) as turn:
            self.turn = turn
            yield turn
        self.turn, self.steps = None, {}
        done = {k: v - first.get(k, 0) for k, v in self.n.items() if v != first.get(k, 0)}
        assert done == steps, (done, steps)
        for k, s in steps.items():
            self.n[k] = first.get(k, 0) + turns * s


def two_blocks(nc, x_in, fm_in, row_in, table_in, mask1_in, mask2_in, pool_in, ws_in, kidx_in,
               wmod0, wmod1, wa, wb, wc, out):
    with ExitStack() as ctx:
        def sem(name):
            return ctx.enter_context(nc.semaphore(name))

        top = [nc.sbuf_base + 127 & ~127]

        def sb(name, shape, dt=F32, at=None):
            size = int(np.prod(shape[1:])) * (2 if dt == BF16 else 4)
            if at is None:
                at = top[0] + 31 & ~31
                top[0] = at + size
            return nc.alloc_sbuf_tensor_at(name, shape, dt, offset=at)

        raw = sb("raw", [P, RING, UNIT])
        hi = sb("hi", [P, RING, UNIT], F32R)
        lo = sb("lo", [P, RING, UNIT], F32R)
        x_at = top[0]
        x = sb("x", [P, TT, D])
        tok_at = top[0]
        tok = sb("tok", [P, 2, TT, N])
        junk_x = sb("junk_x", [P, TT, D], BF16, at=tok_at)
        junk = sb("junk", [P, TT, N], BF16)
        ident = sb("ident", [P, P])
        fm = sb("fm", [P, FM_COLS])
        modfm = sb("modfm", [P, 96])
        fA = sb("fA", [P, KD])
        fG = sb("fG", [P, KD])
        ropeC = sb("ropeC", [P, TT, HD])
        ropeS = sb("ropeS", [P, TT, HD])
        iropeC = sb("iropeC", [P, TT, IROPE])
        iropeS = sb("iropeS", [P, TT, IROPE])
        ones = sb("ones", [P, 1])
        ssq = sb("ssq", [P, TT])
        ssqp = sb("ssqp", [P, TT, 4])
        var = sb("var", [P, TT])
        std = sb("std", [P, TT])
        rstd = sb("rstd", [P, TT])
        stats = sb("stats", [P, TT, 2, 6])
        mv = sb("mv", [P, TT, 2])
        nmax = sb("nmax", [P, TT])
        esum = sb("esum", [P, TT])
        resum = sb("resum", [P, TT])
        best8 = sb("best8", [P, TT, 8])
        sgt = sb("sgt", [P, TT, N])
        h_at = top[0]
        Hh = sb("Hh", [P, KD, T], F32R)
        Hl = sb("Hl", [P, KD, T], F32R)
        free = top[0]
        KB = 1024
        kT = sb("kT", [P, HEADS1, T], at=free)
        v = sb("v", [P, TT, GW], at=free + 8 * KB)
        qT = sb("qT", [P, HEADS1, T], at=free + 16 * KB)
        qidxT = sb("qidxT", [P, IH // 2, T], at=free + 24 * KB)
        O1 = sb("O1", [P, TT, GW], at=free + 24 * KB)
        mergedh = sb("mergedh", [P, KD, T], F32R, at=free)
        mergedl = sb("mergedl", [P, KD, T], F32R, at=free + 16 * KB)
        sg_at = free + 32 * KB
        sg = sb("sg", [P, TT, 2 * D], at=sg_at)
        xn = sb("xn", [P, TT, D], at=sg_at)
        wsT = sb("wsT", [P, 8, P], at=sg_at)
        kT2 = sb("kT2", [P, 2, T], at=sg_at + 4 * KB)
        kn = sb("kn", [P, TT, IDIM], at=sg_at + 6 * KB)
        kr = sb("kr", [P, TT, IROPE], at=sg_at + 6 * KB + 512)
        kidx_gb = sb("kidx_gb", [P, 2, IDIM], at=sg_at + 6 * KB + 768)
        xnT = sb("xnT", [P, KD, T], at=sg_at + 16 * KB)
        ln_g = sb("ln_g", [P, GW], at=sg_at + 24 * KB)
        ln_b = sb("ln_b", [P, GW], at=sg_at + 28 * KB)
        mix = sb("mix", [P, TT, D], at=sg_at)
        q_at = sg_at + 32 * KB
        qlath = sb("qlath", [P, 4, T], F32R, at=q_at)
        qlatl = sb("qlatl", [P, 4, T], F32R, at=q_at + 4 * KB)
        gm1 = sb("gm1", [P, D], at=q_at)
        top[0] = q_at
        score = sb("score", [P, 384])
        work = sb("work", [P, 384])
        top[0] = q_at + 8 * KB
        rl = sb("rl", [P, 2, 512])
        top[0] -= 4 * KB
        kd = sb("kd", [P, TT, P])
        top[0] -= KB
        att1 = sb("att1", [P, 384])
        pt1 = sb("pt1", [P, 384])
        top[0] = q_at + 12 * KB
        selb = sb("selb", [P, 384])
        kx = sb("kx", [P, TT, 80])
        qs = sb("qs", [P, 2, T])
        mask1 = sb("mask1", [P, P])
        mraw = sb("mraw", [P, 2, UNIT])
        macc = sb("macc", [P, 2, N])
        end1 = top[0]
        z = sb("z", [P, TT, D], at=x_at)
        hidh = sb("hidh", [P, FK, T], F32R, at=free)
        hidl = sb("hidl", [P, FK, T], F32R, at=free + FK * T * 4)
        fmix = sb("fmix", [P, TT, D], at=h_at)
        gm2 = sb("gm2", [P, D], at=h_at + 16 * KB)
        zh = sb("zh", [P, KD, T], F32R, at=free)
        zl = sb("zl", [P, KD, T], F32R, at=free + 16 * KB)
        hbh = sb("hbh", [P, KD, T], F32R, at=free + 32 * KB)
        hbl = sb("hbl", [P, KD, T], F32R, at=free + 48 * KB)
        top[0] = free + 64 * KB
        u = sb("u", [P, TT, N])
        ph = sb("ph", [P, 4, T], F32R)
        pl = sb("pl", [P, 4, T], F32R)
        poolM = sb("poolM", [P, 4, 384])
        k2T = sb("k2T", [P, HEADS2, T], at=free)
        v2 = sb("v2", [P, TT, D], at=free + 16 * KB)
        top[0] = free + 64 * KB
        O2 = sb("O2", [P, TT, D])
        top[0] = max(top[0], free + 64 * KB + 4 * KB + 8 * KB + 6 * KB)
        mask2 = sb("mask2", [P, NG, T])
        qTh = sb("qTh", [P, NG, T])
        att2 = sb("att2", [P, NG * 384])
        pt2 = sb("pt2", [P, 384], at=tok_at + TT * N * 4)
        assert max(end1, top[0], free + 2 * FK * T * 4) <= nc.sbuf_usable_end, (
            end1, top[0], free + 2 * FK * T * 4, nc.sbuf_usable_end)

        acc = ctx.enter_context(nc.psum_tensor("acc", [P, 4, N], F32))
        tb = ctx.enter_context(nc.psum_tensor("tb", [P, 4, N], F32))

        const_in = sem("const_in")
        x_loaded = sem("x_loaded")
        row_loaded = sem("row_loaded")
        pool_loaded = sem("pool_loaded")
        mask_loaded = sem("mask_loaded")
        raw_loaded = [sem(f"raw_loaded{i}") for i in range(RING)]
        mod_loaded = [sem(f"mod_loaded{i}") for i in range(2)]
        memory_set = sem("memory_set")
        ws_ready = sem("ws_ready")
        unit_split = sem("unit_split")
        hi_ready = sem("hi_ready")
        unit_used = sem("unit_used")
        acc_free = [sem(f"acc_free{i}") for i in range(4)]
        tb_free = [sem(f"tb_free{i}") for i in range(4)]
        tok_ready = sem("tok_ready")
        tr_split = sem("tr_split")
        tr_hi = sem("tr_hi")
        tr_copy = sem("tr_copy")
        copied = sem("copied")
        in_split = sem("in_split")
        in_scaled = sem("in_scaled")
        in_hi = sem("in_hi")
        var_ready = sem("var_ready")
        std_ready = sem("std_ready")
        ssq_ready = sem("ssq_ready")
        rstd_ready = sem("rstd_ready")
        evac = sem("evac")
        mod_done = sem("mod_done")
        mod_read = sem("mod_read")
        mod_taken = sem("mod_taken")
        gate_ready = sem("gate_ready")
        row_ready = sem("row_ready")
        row_copied = sem("row_copied")
        kidx_ready = sem("kidx_ready")
        kidx_spread = sem("kidx_spread")
        idx_ready = sem("idx_ready")
        relu_ready = sem("relu_ready")
        relu_read = sem("relu_read")
        s_ready = sem("s_ready")
        att_ready = sem("att_ready")
        exp_ready = sem("exp_ready")
        p_ready = sem("p_ready")
        o_ready = sem("o_ready")
        gmlp_ready = sem("gmlp_ready")
        v_normed = sem("v_normed")
        y_ready = sem("y_ready")
        x_ready = sem("x_ready")
        xn_ready = sem("xn_ready")
        out_ready = sem("out_ready")
        dve_chain = sem("dve_chain")
        stored = sem("stored")

        def cols(start, n):
            return bass.ds(start, n) if not isinstance(start, int) else slice(start, start + n)

        def vec(name, k, n=1):
            return fm[:, cols(k + FM[name], n)]

        block = ctx.enter_context(nc.Block())

        @block.sync
        def _(sp):
            sp.dma_start(x[:], x_in).then_inc(x_loaded, 16)
            sp.dma_start(fm[:], fm_in).then_inc(const_in, 16)
            sp.dma_start(ident[:], table_in[:, 0:P]).then_inc(const_in, 16)
            o = P
            for dst, n in ((ropeC, TT * HD), (ropeS, TT * HD), (iropeC, TT * IROPE), (iropeS, TT * IROPE)):
                sp.dma_start(dst[:], table_in[:, o:o + n].rearrange("p (a b) -> p a b", a=TT)).then_inc(const_in, 16)
                o += n
            sp.dma_start(mask1[:], mask1_in).then_inc(const_in, 16)
            c = Counts()

            def load(src):
                s = c.slot("unit", RING)
                if c.n.get("unit", 0) >= RING:
                    sp.wait_ge(unit_split, c.at("unit") - (RING - 1))
                sp.dma_start(raw[:, s, 0:src.shape[-1]], src).then_inc(raw_loaded[s], 16)
                c.up("unit")

            def stream(w, units):
                first = RING if not c.n.get("unit", 0) else 0
                for i in range(first):
                    load(w[i])
                turns = (units - first) // RING
                with c.loop(sp, turns, unit=RING) as turn:
                    for j in range(RING):
                        load(w[bass.ds(turn * RING + (first + j), 1)].rearrange("a p n -> (a p) n"))
                for i in range(first + turns * RING, units):
                    load(w[i])

            stream(wmod0, START_UNITS)
            stream(wa, A_UNITS)
            stream(wb, B_UNITS)
            stream(wc, C_UNITS)
            for tt in range(TT):
                sp.wait_ge(out_ready, tt + 1)
                sp.dma_start(out[tt * P:(tt + 1) * P, :], x[:, tt, :]).then_inc(stored, 16)
            sp.wait_ge(stored, TT * 16)

        @block.gpsimd
        def _(pool):
            pool.memset(ones[:], 1.0).then_inc(memory_set, 1)
            pool.wait_ge(row_loaded, 4 * 16)
            pool.memset(kT2[:], 0.0).then_inc(memory_set, 1)
            pool.affine_select(out=wsT[:], in_=wsT[:], compare_op=ALU.is_ge, fill=0.0, base=0,
                               pattern=[[0, 8], [1, P]], channel_multiplier=-1).then_inc(ws_ready, 1)
            pool.wait_ge(unit_split, START_UNITS - 2 * RING)
            for i in range(2):
                pool.dma_start(mraw[:, i, :], wmod1[i]).then_inc(mod_loaded[i], 16)
            with pool.Fori(0, LATE_BLOCKS * MOD_UNITS // 2 - 1) as n:
                for i in range(2):
                    pool.wait_ge(mod_done, n * 2 + i + 1)
                    pool.dma_start(mraw[:, i, :], wmod1[bass.ds(n * 2 + (i + 2), 1)].rearrange("a p n -> (a p) n"))\
                        .then_inc(mod_loaded[i], 16)

        @block.scalar
        def _(act):
            c = Counts()

            def split(units, n=UNIT):
                for _ in range(units):
                    s = c.slot("unit", RING)
                    act.wait_ge(raw_loaded[s], (c.at("unit", RING) + (START_UNITS // RING + 1)) * 16)
                    act.wait_ge(unit_used, c.at("unit") + 1)
                    act.activation(hi[:, s, 0:n], raw[:, s, 0:n], ACT.Copy).then_inc(hi_ready, 1)
                    c.up("unit")

            def split_to(unit, n=UNIT):
                split(unit - c.n["unit"], n)

            def tile_done(ahead=RING):
                act.wait_ge(unit_used, c.at("unit") + (RING - ahead))

            def root():
                act.wait_ge(var_ready, c.up("var"))
                act.activation(std[:], var[:], ACT.Sqrt).then_inc(std_ready, 1)

            def take_hi(dst, k, b, gain=None, last=True):
                if gain is None:
                    ins = act.activation(dst[:, cols(k, 2), :], tb[:, b, :].rearrange("p (k t) -> p k t", k=2), ACT.Copy)
                else:
                    for j in range(2):
                        ins = act.activation(dst[:, cols(k + j, 1), :], tb[:, b:b + 1, j * T:(j + 1) * T], ACT.Copy,
                                             scale=gain(j))
                if last:
                    ins.then_inc(tr_hi, 1)

            def take_hi_tile(dst, k, gain=None):
                for b in range(2):
                    act.wait_ge(tr_split, c.up("split"))
                    take_hi(dst, k + 2 * b, b, gain and (lambda j, b=b: gain(2 * b + j)))

            def copy_tile(dst, k):
                for b in range(2):
                    act.wait_ge(tr_copy, c.up("copy"))
                    act.activation(dst[:, cols(k + 2 * b, 2), :], tb[:, b, :].rearrange("p (k t) -> p k t", k=2),
                                   ACT.Copy).then_inc(tb_free[b], 1)

            def read_out(dst_of, pair, func=ACT.Copy, scaled=False):
                for tt in range(TT):
                    ins = act.activation(dst_of(tt), acc[:, 2 * pair + tt, :], func,
                                         scale=rstd[:, tt:tt + 1] if scaled else 1.0)
                    ins.then_inc(acc_free[2 * pair + tt], 1)

            def square_tile(pair, col):
                tile_done()
                for tt in range(TT):
                    act.activation(junk[:, tt, :], acc[:, 2 * pair + tt, :], ACT.Square,
                                   accum_out=ssqp[:, tt, cols(col, 1)]).then_inc(evac, 1)

            def spread_rows(dst):
                for q in range(4):
                    act.wait_ge(row_ready, c.up("row"))
                    act.activation(dst[:, q * N:(q + 1) * N], tb[:, 2, :], ACT.Copy).then_inc(tb_free[2], 1)

            def square_x():
                for tt in range(TT):
                    act.wait_ge(x_ready, c.up("x"))
                    ins = act.activation(junk_x[:, tt, :], x[:, tt, :], ACT.Square,
                                         accum_out=ssq[:, tt:tt + 1])
                ins.then_inc(ssq_ready, 1)

            act.wait_ge(x_loaded, 16)
            for tt in range(TT):
                ins = act.activation(xn[:, tt, :], x[:, tt, :], ACT.Square, accum_out=ssq[:, tt:tt + 1])
            ins.then_inc(ssq_ready, 1)
            root()
            for k in range(KD // 2):
                act.wait_ge(tr_copy, c.up("copy"))
                act.activation(xnT[:, 2 * k:2 * k + 2, :], tb[:, k % 3, :].rearrange("p (k t) -> p k t", k=2), ACT.Copy)\
                    .then_inc(tb_free[k % 3], 1)
            for q in range(4):
                act.wait_ge(in_scaled, q + 1)
                act.activation(Hh[:, 4 * q:4 * q + 4, :], xnT[:, 4 * q:4 * q + 4, :], ACT.Copy).then_inc(in_hi, 1)
                if q % 2:
                    split(2)
            act.wait_ge(in_split, 4)
            act.dma_start(wsT[:], ws_in).then_inc(row_loaded, 16)
            act.dma_start(kidx_gb[:], kidx_in).then_inc(row_loaded, 16)
            for i, row in enumerate((ln_g, ln_b)):
                act.dma_start(row[:], row_in[i].partition_broadcast(P))\
                    .then_inc(row_loaded, 16)

            split_to(8)
            split_to(10, 640)
            split_to(12)
            tile_done()
            for tt in range(TT):
                ins = act.activation(junk[:, tt, :], acc[:, tt, :], ACT.Square, accum_out=ssq[:, tt:tt + 1])
            ins.then_inc(ssq_ready, 1)
            root()
            take_hi_tile(qlath, 0, lambda j: vec("qlat_g", j))
            split_to(14)
            tile_done()
            for tt in range(TT):
                act.activation(kx[:, tt, :], acc[:, 2 + tt, 0:80], ACT.Copy).then_inc(acc_free[2 + tt], 1)
            root()
            split_to(22)
            act.wait_ge(kidx_ready, 1)
            act.wait_ge(memory_set, 2)
            act.wait_ge(tr_copy, c.up("copy"))
            act.activation(kT2[0:64, 0, :], tb[0:64, 2, 0:T], ACT.Copy)
            act.activation(kT2[64:128, 1, :], tb[64:128, 2, 0:T], ACT.Copy).then_inc(tb_free[2], 1)
            copy_tile(kT, 0)
            split_to(30)
            copy_tile(kT, 4)
            split_to(32)
            copy_tile(qidxT, 0)
            split_to(34)
            copy_tile(qidxT, 4)
            split_to(36)
            copy_tile(qT, 0)
            split_to(38)
            copy_tile(qT, 4)
            for q in range(IH):
                split_to(40 + q)
                if 40 + q == 46:
                    tile_done()
                    read_out(lambda tt: v[:, tt, 0:N], 0)
                if 40 + q == 54:
                    tile_done()
                    read_out(lambda tt: v[:, tt, N:2 * N], 1)
                act.wait_ge(idx_ready, q + 1)
                if q >= 2:
                    act.wait_ge(relu_read, q - 1)
                w = P if q % 2 == 0 else T
                act.activation(rl[:, q % 2, 0:2 * w], tb[:, q % 2, 0:2 * w], ACT.Relu).then_inc(relu_ready, 1)
            for n in range(4):
                split_to(62 + 8 * n)
                tile_done()
                read_out(lambda tt: z[:, tt, n * N:(n + 1) * N], n % 2, ACT.Gelu_apprx_tanh)
                if n == 1:
                    root()
            with c.loop(act, HEADS1 // 2, unit=16, att=2, copy=2) as turn:
                for e in range(2):
                    head = turn * 2 + e
                    act.activation(qs[:, e, :], qT[:, cols(head, 1), :].rearrange("p a t -> p (a t)"), ACT.Copy)\
                        .then_inc(copied, 1)
                    split(2)
                    act.wait_ge(att_ready, c.up("att"))
                    act.activation(att1[:, 0:T], att1[:, 0:T], ACT.Exp, bias=nmax[:, 1:2], accum_out=esum[:, 1:2])
                    act.activation(att1[:, T:T + P], att1[:, T:T + P], ACT.Exp, bias=nmax[:, 0:1],
                                   accum_out=esum[:, 0:1]).then_inc(exp_ready, 1)
                    split(2)
                    act.wait_ge(tr_copy, c.up("copy"))
                    act.activation(pt1[:], tb[:, 1, 0:384], ACT.Copy).then_inc(tb_free[1], 1)
                    split(4)
                    tile_done()
                    read_out(lambda tt: sg[:, tt, cols(head * N, N)], e, ACT.Sigmoid)
            take_hi_tile(Hh, 0)
            take_hi_tile(Hh, 4)
            act.dma_start(x[:], x_in).then_inc(x_loaded, 16)
            split(2)
            take_hi_tile(Hh, 8)
            split(2)
            take_hi_tile(Hh, 12)
            spread_rows(gm1)
            split(4)
            take_hi_tile(mergedh, 0)
            with c.loop(act, 3, unit=8, split=2) as j:
                split(8)
                take_hi_tile(mergedh, j * 4 + 4)
            with c.loop(act, 2, unit=16) as i:
                for e in range(2):
                    split(8)
                    square_tile(e, i * 2 + e)
            root()
            square_x()
            root()
            for k in range(KD // 2):
                act.wait_ge(tr_split, c.up("split"))
                for j in range(2):
                    ins = act.activation(Hh[:, 2 * k + j, :], tb[:, k % 4, j * T:(j + 1) * T], ACT.Identity,
                                         scale=fA[:, 2 * k + j:2 * k + j + 1],
                                         bias=modfm[:, SHIFT_F + 2 * k + j:SHIFT_F + 2 * k + j + 1])
                ins.then_inc(tr_hi, 1)
            with c.loop(act, FT, unit=16, split=2) as n:
                split(8)
                tile_done()
                read_out(lambda tt: sgt[:, tt, :], 0, ACT.Silu)
                split(8)
                take_hi_tile(hidh, n * 4)
            spread_rows(gm2)
            with c.loop(act, 2, unit=FK) as i:
                for e in range(2):
                    split(FK // 2)
                    square_tile(e, i * 2 + e)
            root()
            for k in range(KD // 2):
                act.wait_ge(tr_split, c.up("split"))
                take_hi(Hh, 2 * k, k % 4, lambda j: vec("norm_a", 2 * k + j))
            act.dma_start(poolM[:], pool_in).then_inc(pool_loaded, 16)
            act.dma_start(mask2[:], mask2_in).then_inc(mask_loaded, 16)
            square_x()
            root()
            act.wait_ge(rstd_ready, c.at("var"))
            with c.loop(act, 4, unit=20, split=4) as g:
                split(8)
                tile_done()
                read_out(lambda tt: u[:, tt, :], 0, scaled=True)
                for b in range(2):
                    act.wait_ge(tr_split, c.up("split"))
                    take_hi(ph, 2 * b, 2 + b)
                split(4)
                split(4, N)
                tile_done()
                read_out(lambda tt: sgt[:, tt, :], 1, ACT.Silu, scaled=True)
                split(4)
                take_hi_tile(zh, g * 4, lambda j: vec("scale_a", g * 4 + j))
            c.n["acc0"] = c.n["acc1"] = TILES_BEFORE_OUT_A // 2
            with c.loop(act, 2, unit=16, split=4, acc0=1, acc1=1) as i:
                for e in range(2):
                    split(8)
                    n = c.up(f"acc{e}")
                    for tt in range(TT):
                        act.wait_ge(acc_free[2 * e + tt], n + 1)
                        act.activation(x[:, tt, cols((i * 2 + e) * N, N)], tok[:, e, tt, :], ACT.Copy)
                        ins = act.activation(junk[:, tt, :], tok[:, e, tt, :], ACT.Square, accum_out=ssqp[:, tt, cols(i * 2 + e, 1)])
                    ins.then_inc(evac, 1)
                    for b in range(2):
                        act.wait_ge(tr_split, c.up("split"))
                        k = (i * 2 + e) * 4 + 2 * b
                        take_hi(Hh, k, b, lambda j: vec("norm_kv", k + j), last=False)
                        take_hi(hbh, k, b, lambda j: vec("norm_b", k + j))
            root()
            act.wait_ge(rstd_ready, c.at("var"))
            with c.loop(act, 4, unit=16, copy=2) as i:
                split(8)
                copy_tile(k2T, i * 4)
                split(8)
                tile_done()
                read_out(lambda tt: v2[:, tt, cols(i * N, N)], 1, scaled=True)
            W = 2 * HN

            def attention(now=W, ahead=W):
                split(2, now)
                for b, k, nk in ((0, 0, 2), (1, 2, 1)):
                    act.wait_ge(tr_copy, c.up("copy"))
                    act.activation(qTh[:, k:k + nk, :], tb[:, b, 0:nk * T].rearrange("p (k t) -> p k t", k=nk), ACT.Copy)\
                        .then_inc(tb_free[b], 1)
                split(2, now)
                act.wait_ge(att_ready, c.up("att"))
                act.activation(att2[:, 0:NG * T], att2[:, 0:NG * T], ACT.Exp, bias=nmax[:, 1:2], accum_out=esum[:, 1:2])
                act.activation(att2[:, NG * T:], att2[:, NG * T:], ACT.Exp, bias=nmax[:, 0:1],
                               accum_out=esum[:, 0:1]).then_inc(exp_ready, 1)
                split(2, ahead)
                act.wait_ge(tr_copy, c.up("copy"))
                act.activation(pt2[:], tb[:, 3, 0:384], ACT.Copy).then_inc(tb_free[3], 1)
                split(2, ahead)

            split(8, W)
            with c.loop(act, HEADS2 // 2 - 1, unit=16, copy=6, att=2):
                for e in range(2):
                    attention()
            attention(W, UNIT)
            for i in range(4):
                if i == 0:
                    attention(UNIT, UNIT)
                else:
                    split(8)
                tile_done()
                read_out(lambda tt: sgt[:, tt, :], i % 2, ACT.Silu, scaled=True)
                take_hi_tile(Hh, 4 * i)
            c.n["acc0"] = c.n["acc1"] = TILES_BEFORE_OUT_B // 2
            for i in range(4):
                split(8 if i < 3 else 4)
                n = c.up(f"acc{i % 2}")
                for tt in range(TT):
                    act.wait_ge(acc_free[2 * (i % 2) + tt], n + 1)
                    ins = act.activation(junk[:, tt, :], x[:, tt, i * N:(i + 1) * N], ACT.Square, accum_out=ssqp[:, tt, i:i + 1])
                ins.then_inc(evac, 1)
            root()

        @block.vector
        def _(dve):
            c = Counts()

            def chain(ins):
                ins.then_inc(dve_chain, 1)
                dve.wait_ge(dve_chain, c.up("chain"))

            def split(units, n=UNIT, mod=False):
                for _ in range(units):
                    s = c.slot("unit", RING)
                    dve.wait_ge(hi_ready, c.up("unit"))
                    dve.tensor_tensor(lo[:, s, 0:n], raw[:, s, 0:n], hi[:, s, 0:n].bitcast(F32), ALU.subtract)\
                        .then_inc(unit_split, 1)
                    if mod:
                        late_unit()

            def split_to(unit, n=UNIT, mod=False):
                split(unit - c.n["unit"], n, mod)

            def tile_done(ahead=RING):
                dve.wait_ge(unit_used, c.at("unit") + (RING - ahead))

            def multiply_add(b, j, src, done):
                for kk in range(2):
                    w, ck = src[:, kk * N:(kk + 1) * N], vec("c", 2 * j + kk)
                    if j == kk == 0:
                        ins = dve.tensor_scalar(macc[:, b, :], w, ck, None, ALU.mult)
                    else:
                        ins = dve.scalar_tensor_tensor(macc[:, b, :], w, ck, macc[:, b, :], ALU.mult, ALU.add)
                    if kk == 0:
                        chain(ins)
                    else:
                        done(ins)

            def late_unit():
                s, j = c.slot("late", 2), c.slot("late", MOD_UNITS)
                b = c.slot("late", 2 * MOD_UNITS) // MOD_UNITS
                if j == 0:
                    dve.wait_ge(mod_read, c.at("late", MOD_UNITS) + (START_BLOCKS + 1))
                dve.wait_ge(mod_loaded[s], c.at("late", 2) * 16 + 16)

                def done(ins):
                    ins.then_inc(mod_done, 1)
                    dve.wait_ge(mod_done, c.up("late"))

                multiply_add(b, j, mraw[:, s, :], done)

            def take_mod(start, n, blocks):
                dve.wait_ge(mod_read, blocks + 2)
                dve.tensor_tensor(modfm[:, start:start + n], tb[:, 3, start:start + n], vec("b_mod", start, n), ALU.add)\
                    .then_inc(mod_taken, 1)
                dve.wait_ge(mod_taken, c.up("taken"))

            def gated_gain(gate, gain):
                dve.tensor_tensor(fG[:], modfm[:, gate:gate + KD], vec(gain, 0, KD), ALU.mult).then_inc(gate_ready, 1)

            def inverse_root():
                dve.wait_ge(std_ready, c.up("std"))
                dve.reciprocal(rstd[:], std[:]).then_inc(rstd_ready, 1)
                dve.wait_ge(rstd_ready, c.n["std"])

            def rms(n):
                dve.tensor_scalar(var[:], ssq[:], 1.0 / n, EPS, ALU.mult, ALU.add).then_inc(var_ready, 1)
                inverse_root()

            def sum_squares():
                chain(dve.tensor_reduce(ssq[:], ssqp[:], AX_X, ALU.add))

            def layer_norm_stats(src, chunks):
                for tt in range(TT):
                    for i, chunk in enumerate(chunks):
                        ins = dve.bn_stats(stats[:, tt, i, :], src(tt, chunk))
                chain(ins)
                for tt in range(TT):
                    ins = dve.bn_aggr(mv[:, tt, :], stats[:, tt, 0:len(chunks), :])
                chain(ins)
                dve.tensor_scalar(var[:], mv[:, :, 1:2].rearrange("p t a -> p (t a)"), EPS, None, ALU.add)\
                    .then_inc(var_ready, 1)
                inverse_root()

            def rotate(pair, dst, heads, dim, half, cos, sin, width=N):
                h4 = lambda ap: ap.rearrange("p (h d) -> p h d", h=heads)
                spread = lambda ap: ap.unsqueeze(1).to_broadcast([P, heads, ap.shape[-1]])
                rot = 2 * half
                for tt in range(TT):
                    src, tmp, o = h4(acc[:, 2 * pair + tt, 0:width]), h4(sgt[:, tt, 0:width]), h4(dst(tt))
                    ins = dve.tensor_tensor(tmp[:, :, 0:half], src[:, :, half:rot], spread(sin[:, tt, 0:half]), ALU.mult)
                    if tt == 1:
                        chain(ins)
                    dve.tensor_tensor(tmp[:, :, half:rot], src[:, :, 0:half], spread(sin[:, tt, half:rot]), ALU.mult)
                    ins = dve.tensor_tensor(o[:, :, 0:rot], src[:, :, 0:rot], spread(cos[:, tt, 0:rot]), ALU.mult)
                    if rot < dim:
                        ins = dve.tensor_copy(o[:, :, rot:dim], src[:, :, rot:dim])
                    ins.then_inc(acc_free[2 * pair + tt], 1)
                for tt in range(TT):
                    tmp, o = h4(sgt[:, tt, 0:width]), h4(dst(tt))
                    ins = dve.tensor_tensor(o[:, :, 0:rot], o[:, :, 0:rot], tmp[:, :, 0:rot], ALU.add)
                    if tt == 0:
                        chain(ins)
                ins.then_inc(tok_ready, 1)

            def take_lo(dst, src_hi, k, b, gain=None, last=True):
                if gain is None:
                    ins = dve.tensor_tensor(dst[:, cols(k, 2), :], tb[:, b, :].rearrange("p (k t) -> p k t", k=2),
                                            src_hi[:, cols(k, 2), :].bitcast(F32), ALU.subtract)
                else:
                    for j in range(2):
                        ins = dve.scalar_tensor_tensor(dst[:, cols(k + j, 1), :], tb[:, b:b + 1, j * T:(j + 1) * T], gain(j),
                                                       src_hi[:, cols(k + j, 1), :].bitcast(F32), ALU.mult, ALU.subtract)
                if last:
                    ins.then_inc(tb_free[b], 1)

            def take_lo_tile(dst, src_hi, k, gain=None, banks=(0, 1)):
                for i, b in enumerate(banks):
                    dve.wait_ge(tr_hi, c.up("hi"))
                    take_lo(dst, src_hi, k + 2 * i, b, gain and (lambda j, i=i: gain(2 * i + j)))

            def masked_scores(att, parts, tokens):
                for dst, scores, mask, free in parts:
                    ins = dve.scalar_tensor_tensor(dst, scores, SCALE, mask, ALU.mult, ALU.add)
                    if free is not None:
                        ins.then_inc(free, 1)
                    else:
                        chain(ins)
                for i, (tt, at) in enumerate(tokens):
                    ins = dve.tensor_reduce(nmax[:, tt:tt + 1], att[:, at], AX_X, ALU.max, negate=True)
                    if i == 0:
                        chain(ins)
                ins.then_inc(att_ready, 1)

            dve.wait_ge(const_in, 7 * 16)
            dve.wait_ge(x_loaded, 16)
            dve.wait_ge(ssq_ready, c.up("ssq"))
            rms(D)
            for tt in range(TT):
                dve.tensor_scalar(xn[:, tt, :], x[:, tt, :], rstd[:, tt:tt + 1], None, ALU.mult).then_inc(xn_ready, 1)
            with c.loop(dve, START_BLOCKS // 2, start=2 * MOD_UNITS, chain=2 * MOD_UNITS):
                for b in range(2):
                    dve.wait_ge(mod_read, c.at("start", MOD_UNITS) + 1)
                    for j in range(MOD_UNITS):
                        s = c.slot("start", RING)
                        dve.wait_ge(raw_loaded[s], c.at("start", RING) * 16 + 16)

                        def done(ins):
                            ins.then_inc(unit_split, 1)
                            dve.wait_ge(unit_split, c.up("start"))

                        multiply_add(b, j, raw[:, s, :], done)
            take_mod(0, 4 * START_BLOCKS, START_BLOCKS)
            in_mod = modfm[:, 0:4 * START_BLOCKS].rearrange("p (b s k) -> p b s k", s=2, k=4)
            chain(dve.scalar_tensor_tensor(fA[:].rearrange("p (b k) -> p b k", k=4), in_mod[:, :, 0, :], 1.0,
                                           vec("g_pre_mix", 0, KD).rearrange("p (b k) -> p b k", k=4), ALU.add, ALU.mult))
            for b in range(3):
                dve.wait_ge(tb_free[b], 1 + len(range(b, KD // 2, 3)))

            def scale_in(q):
                for k in range(4 * q, 4 * q + 4):
                    ins = dve.tensor_scalar(xnT[:, k, :], xnT[:, k, :], fA[:, k:k + 1], in_mod[:, q, 1, k % 4:k % 4 + 1],
                                            ALU.mult, ALU.add)
                ins.then_inc(in_scaled, 1)

            def split_in(q):
                k = slice(4 * q, 4 * q + 4)
                dve.wait_ge(in_hi, q + 1)
                dve.tensor_tensor(Hl[:, k, :], xnT[:, k, :], Hh[:, k, :].bitcast(F32), ALU.subtract).then_inc(in_split, 1)

            scale_in(0)
            scale_in(1)
            split_in(0)
            scale_in(2)
            split_in(1)
            split(2)
            scale_in(3)
            split_in(2)
            split_in(3)
            split(2)

            split_to(8)
            split_to(10, 640)
            split_to(12)
            dve.wait_ge(ssq_ready, c.up("ssq"))
            rms(QLAT)
            for tt in range(TT):
                dve.tensor_scalar(tok[:, 0, tt, :], acc[:, tt, :], rstd[:, tt:tt + 1], None, ALU.mult)\
                    .then_inc(acc_free[tt], 1)
            take_lo_tile(qlatl, qlath, 0, lambda j: vec("qlat_g", j))
            split_to(14)
            for tt in range(TT):
                dve.wait_ge(acc_free[2 + tt], 2)
            layer_norm_stats(lambda tt, _: kx[:, tt, 0:IDIM], (0,))
            for tt in range(TT):
                ins = dve.tensor_scalar(kn[:, tt, :], kx[:, tt, 0:IDIM], mv[:, tt, 0:1], rstd[:, tt:tt + 1],
                                        ALU.subtract, ALU.mult)
            chain(ins)
            dve.wait_ge(row_loaded, 4 * 16)
            both = lambda i: kidx_gb[:, i:i + 1, :].to_broadcast([P, TT, IDIM])
            chain(dve.tensor_tensor(kn[:], kn[:], both(0), ALU.mult))
            chain(dve.tensor_tensor(kn[:], kn[:], both(1), ALU.add))
            ih = IROPE // 2
            dve.tensor_tensor(kr[:, :, 0:ih], kn[:, :, ih:IROPE], iropeS[:, :, 0:ih], ALU.mult)
            dve.tensor_tensor(kr[:, :, ih:IROPE], kn[:, :, 0:ih], iropeS[:, :, ih:IROPE], ALU.mult)
            dve.tensor_copy(kd[:, :, IROPE:IDIM], kn[:, :, IROPE:IDIM])
            chain(dve.tensor_tensor(kd[:, :, 0:IROPE], kn[:, :, 0:IROPE], iropeC[:], ALU.mult))
            chain(dve.tensor_tensor(kd[:, :, 0:IROPE], kd[:, :, 0:IROPE], kr[:], ALU.add))
            dve.tensor_scalar(kx[:, :, IDIM:], kx[:, :, IDIM:], IDX_SCALE, None, ALU.mult)
            dve.tensor_copy(kd[:, :, IDIM:], kd[:, :, 0:IDIM]).then_inc(kidx_ready, 1)
            split_to(22, mod=True)
            tile_done()
            rotate(0, lambda tt: tok[:, 1, tt, :], 4, HD, HD // 2, ropeC, ropeS)
            split_to(30)
            tile_done()
            rotate(1, lambda tt: tok[:, 0, tt, :], 4, HD, HD // 2, ropeC, ropeS)
            for t in range(4):
                split_to(32 + 2 * t)
                tile_done()
                dve.wait_ge(tr_copy, K_COPIED + 2 * t)
                tile = lambda tt: tok[:, (t + 1) % 2, tt, :]
                if t < 2:
                    rotate(t % 2, tile, 8, IDIM, IROPE // 2, iropeC, iropeS)
                else:
                    rotate(t % 2, tile, 4, HD, HD // 2, ropeC, ropeS)
            keys = (slice(T, T + P), slice(0, T))

            for q in range(IH):
                split_to(40 + q, mod=40 + q > 42 and 40 + q <= 50)
                tt, h = q % 2, q - q % 2
                w = P if tt == 0 else T
                dve.wait_ge(relu_ready, q + 1)
                weight = lambda j: kx[:, tt, IDIM + h + j:IDIM + h + j + 1]
                if h == 0:
                    ins = dve.tensor_scalar(score[:, keys[tt]], rl[:, tt, 0:w], weight(0), None, ALU.mult)
                else:
                    ins = dve.scalar_tensor_tensor(score[:, keys[tt]], rl[:, tt, 0:w], weight(0), score[:, keys[tt]],
                                                   ALU.mult, ALU.add)
                chain(ins)
                dve.scalar_tensor_tensor(score[:, keys[tt]], rl[:, tt, w:2 * w], weight(1), score[:, keys[tt]],
                                         ALU.mult, ALU.add).then_inc(relu_read, 1)
            split_to(57, mod=True)
            dve.wait_ge(relu_read, IH)
            diagonal = (slice(T, T + P), slice(P, T))
            for tt in range(TT):
                ins = dve.tensor_tensor(score[:, diagonal[tt]], score[:, diagonal[tt]], mask1[:], ALU.add)
            chain(ins)
            left = score
            for r in range(TOPK // 8):
                for tt in range(TT):
                    ins = dve.max(best8[:, tt, :], left[:, keys[tt]])
                chain(ins)
                for tt in range(TT):
                    ins = dve.match_replace(work[:, keys[tt]], best8[:, tt, :], left[:, keys[tt]], TAKEN)
                chain(ins)
                left = work
                split_to(58 + r, mod=r < 6)
            chain(dve.tensor_scalar(selb[:], work[:], TAKEN, -BIG, ALU.not_equal, ALU.mult))
            for tt in range(TT):
                ins = dve.tensor_tensor(selb[:, diagonal[tt]], selb[:, diagonal[tt]], mask1[:], ALU.add)
            split_to(70)
            for tt in range(TT):
                dve.wait_ge(acc_free[2 + tt], 11 // 2 + 2)
            layer_norm_stats(lambda tt, i: z[:, tt, i * N:(i + 1) * N], (0, 1))
            for tt in range(TT):
                ins = dve.tensor_scalar(z[:, tt, 0:GW], z[:, tt, 0:GW], mv[:, tt, 0:1], rstd[:, tt:tt + 1],
                                        ALU.subtract, ALU.mult)
                chain(ins)
            dve.wait_ge(row_loaded, 4 * 16)
            for row, op in ((ln_g, ALU.mult), (ln_b, ALU.add)):
                for tt in range(TT):
                    ins = dve.tensor_tensor(z[:, tt, 0:GW], z[:, tt, 0:GW], row[:], op)
                    if row is ln_g:
                        chain(ins)
            ins.then_inc(v_normed, 1)

            def gate_u(first):
                for g in range(first, first + 4):
                    b = g // 2 % 2
                    if g % 2 == 0:
                        dve.wait_ge(gmlp_ready, c.up("gmlp"))
                    ug = z[:, :, GW + g * P:GW + (g + 1) * P]
                    ins = dve.scalar_tensor_tensor(ug, tb[:, b, (g % 2) * T:(g % 2 + 1) * T].rearrange("p (t d) -> p t d", t=TT),
                                                   vec("b_s", g), ug, ALU.add, ALU.mult)
                    if g % 2 == 1:
                        ins.then_inc(tb_free[b], 1)

            split_to(72)
            split_to(80, mod=True)
            for tt in range(TT):
                dve.wait_ge(acc_free[tt], 12 // 2 + 2)
            gate_u(0)
            split_to(86)
            for tt in range(TT):
                dve.wait_ge(acc_free[2 + tt], 13 // 2 + 2)
            gate_u(4)
            with c.loop(dve, HEADS1 // 2, unit=16, late=2 * MOD_UNITS, s=2, exp=2, o=2, chain=2 * (MOD_UNITS + 3)) as turn:
                for e in range(2):
                    head = turn * 2 + e
                    split(2, mod=True)
                    dve.wait_ge(s_ready, c.up("s"))
                    masked_scores(att1, [(att1[:, keys[tt]], tb[:, 0, keys[tt]], selb[:, keys[tt]], tb_free[0] if tt else None)
                                         for tt in range(TT)], [(tt, keys[tt]) for tt in range(TT)])
                    split(4, mod=True)
                    dve.wait_ge(exp_ready, c.up("exp"))
                    chain(dve.reciprocal(resum[:], esum[:]))
                    dve.wait_ge(o_ready, c.up("o"))
                    for tt in range(TT):
                        ins = dve.tensor_scalar(O1[:, tt, cols(head * HD, HD)], tb[:, 2, tt * P:(tt + 1) * P],
                                                resum[:, tt:tt + 1], None, ALU.mult)
                    ins.then_inc(tb_free[2], 1)
                    split(2, mod=True)
            take_lo_tile(Hl, Hh, 0)
            take_lo_tile(Hl, Hh, 4)
            take_mod(GATE_M, 3 * KD, START_BLOCKS + 12)
            gated_gain(GATE_M, "g_post_mix")
            dve.scalar_tensor_tensor(fA[:], modfm[:, SCALE_F:SCALE_F + KD], 1.0, vec("g_pre_ffn", 0, KD), ALU.add, ALU.mult)
            split(2)
            take_lo_tile(Hl, Hh, 8)
            split(2)
            take_lo_tile(Hl, Hh, 12)

            def merge_a(j):
                tile_done()
                for tt in range(TT):
                    dve.tensor_tensor(tok[:, 0, tt, :], acc[:, tt, :], sg[:, tt, cols(j * N, N)], ALU.mult)\
                        .then_inc(acc_free[tt], 1)

            def merge_b(j):
                tile_done()
                for tt in range(TT):
                    dve.tensor_tensor(sgt[:, tt, :], acc[:, 2 + tt, :], sg[:, tt, cols(j * N + D, N)], ALU.mult)\
                        .then_inc(acc_free[2 + tt], 1)
                for tt in range(TT):
                    dve.wait_ge(acc_free[2 + tt], j + (TILES_BEFORE_MERGE // 2 + 2))
                    ins = dve.tensor_tensor(tok[:, 0, tt, :], tok[:, 0, tt, :], sgt[:, tt, :], ALU.add)
                ins.then_inc(tok_ready, 1)
                take_lo_tile(mergedl, mergedh, j * 4)

            merge_a(0)
            split(4)
            merge_b(0)
            with c.loop(dve, 3, unit=8, hi=2) as j:
                split(4)
                merge_a(j + 1)
                split(4)
                merge_b(j + 1)

            def gated_tile(dst, gains, pair, col):
                for tt in range(TT):
                    dve.wait_ge(evac, c.up("evac"))
                    dve.tensor_tensor(dst[:, tt, cols(col, N)], acc[:, 2 * pair + tt, :], gains[:, cols(col, N)], ALU.mult)\
                        .then_inc(acc_free[2 * pair + tt], 1)

            def add_normed(src):
                sum_squares()
                rms(D)
                for tt in range(TT):
                    dve.scalar_tensor_tensor(x[:, tt, :], src[:, tt, :], rstd[:, tt:tt + 1], x[:, tt, :], ALU.mult, ALU.add)\
                        .then_inc(x_ready, 1)

            with c.loop(dve, 2, unit=16, evac=4, late=2 * MOD_UNITS, chain=2 * MOD_UNITS) as i:
                for e in range(2):
                    split(8, mod=True)
                    gated_tile(mix, gm1, e, (i * 2 + e) * N)
            dve.wait_ge(x_loaded, 2 * 16)
            add_normed(mix)
            take_mod(GATE_F, KD, START_BLOCKS + LATE_BLOCKS)
            gated_gain(GATE_F, "g_post_ffn")
            dve.wait_ge(ssq_ready, c.up("ssq"))
            rms(D)
            for tt in range(TT):
                dve.tensor_scalar(mix[:, tt, :], x[:, tt, :], rstd[:, tt:tt + 1], None, ALU.mult).then_inc(xn_ready, 1)
            for k in range(KD // 2):
                dve.wait_ge(tr_hi, c.up("hi"))
                for j in range(2):
                    kt = 2 * k + j
                    ins = dve.tensor_scalar(sgt[:, k % 2, j * T:(j + 1) * T], tb[:, k % 4, j * T:(j + 1) * T], fA[:, kt:kt + 1],
                                            modfm[:, SHIFT_F + kt:SHIFT_F + kt + 1], ALU.mult, ALU.add)
                chain(ins)
                dve.tensor_tensor(Hl[:, 2 * k:2 * k + 2, :], sgt[:, k % 2, :].rearrange("p (k t) -> p k t", k=2),
                                  Hh[:, 2 * k:2 * k + 2, :].bitcast(F32), ALU.subtract).then_inc(tb_free[k % 4], 1)

            with c.loop(dve, FT, unit=16, hi=2) as n:
                split(16)
                tile_done()
                for tt in range(TT):
                    dve.tensor_tensor(tok[:, 0, tt, :], acc[:, 2 + tt, :], sgt[:, tt, :], ALU.mult).then_inc(acc_free[2 + tt], 1)
                take_lo_tile(hidl, hidh, n * 4)
            with c.loop(dve, 2, unit=FK, evac=4) as i:
                for e in range(2):
                    split(FK // 2)
                    gated_tile(fmix, gm2, e, (i * 2 + e) * N)
            add_normed(fmix)
            for k in range(KD // 2):
                dve.wait_ge(tr_hi, c.up("hi"))
                take_lo(Hl, Hh, 2 * k, k % 4, lambda j: vec("norm_a", 2 * k + j))
            dve.wait_ge(ssq_ready, c.up("ssq"))
            rms(D)
            with c.loop(dve, 4, unit=20, hi=4) as g:
                split(8)
                take_lo_tile(pl, ph, 0, banks=(2, 3))
                split(4)
                split(4, N)
                split(4)
                tile_done()
                for tt in range(TT):
                    dve.tensor_tensor(tok[:, 1, tt, :], tb[:, 2 + tt, :], sgt[:, tt, :], ALU.mult).then_inc(tb_free[2 + tt], 1)
                take_lo_tile(zl, zh, g * 4, lambda j: vec("scale_a", g * 4 + j))
            with c.loop(dve, 2, unit=16, hi=4) as i:
                for e in range(2):
                    split(8)
                    tile_done()
                    t = i * 2 + e
                    for tt in range(TT):
                        dve.tensor_tensor(tok[:, e, tt, :], acc[:, 2 * e + tt, :], x[:, tt, cols(t * N, N)], ALU.add)\
                            .then_inc(acc_free[2 * e + tt], 1)
                    for b in range(2):
                        k = t * 4 + 2 * b
                        dve.wait_ge(tr_hi, c.up("hi"))
                        take_lo(Hl, Hh, k, b, lambda j: vec("norm_kv", k + j), last=False)
                        take_lo(hbl, hbh, k, b, lambda j: vec("norm_b", k + j))
            dve.wait_ge(evac, c.up("evac", 4))
            sum_squares()
            rms(D)
            for table in (ropeC, ropeS):
                for tt in range(TT):
                    ins = dve.tensor_scalar(table[:, tt, :], table[:, tt, :], rstd[:, tt:tt + 1], None, ALU.mult)
            chain(ins)
            c.n["copy"] = COPIES_BEFORE_K2
            with c.loop(dve, 4, unit=16, copy=2, chain=2):
                split(8)
                tile_done()
                dve.wait_ge(tr_copy, c.at("copy"))
                c.up("copy", 2)
                rotate(0, lambda tt: tok[:, 0, tt, :], 4, HD, HD // 2, ropeC, ropeS)
                split(8)
            dve.wait_ge(mask_loaded, 16)
            S1 = NG * T

            def turn_queries(pair):
                tile_done()
                rotate(pair, lambda tt: tok[:, 0, tt, 0:HN], NG, HD, HD // 2, ropeC, ropeS, HN)

            def attention(head, pair=None, now=2 * HN, ahead=2 * HN):
                split(4, now)
                dve.wait_ge(s_ready, c.up("s"))
                by_group = lambda ap: ap.rearrange("p (g t) -> p g t", t=P)
                masked_scores(att2, (
                    (att2[:, 0:2 * T], tb[:, 0, :], mask2[:, 0:2, :].rearrange("p g t -> p (g t)"), tb_free[0]),
                    (att2[:, 2 * T:S1], tb[:, 1, 0:T], mask2[:, 2, :], tb_free[1]),
                    (att2[:, S1:S1 + P], tb[:, 2, 0:P], mask2[:, 0, P:T], None),
                    (by_group(att2[:, S1 + P:]), by_group(tb[:, 2, P:NG * P]), mask2[:, 1:, P:T], tb_free[2])),
                    ((1, slice(0, S1)), (0, slice(S1, S1 + NG * P))))
                dve.wait_ge(exp_ready, c.up("exp"))
                dve.reciprocal(resum[:], esum[:])
                for g in range(1, NG):
                    for at, w in ((0, T), (S1, P)):
                        ins = dve.tensor_tensor(att2[:, at:at + w], att2[:, at:at + w], att2[:, at + g * w:at + (g + 1) * w],
                                                ALU.add)
                        if g == 1 and at:
                            chain(ins)
                ins.then_inc(p_ready, 1)
                split(4, ahead)
                if pair is not None:
                    turn_queries(pair)
                dve.wait_ge(o_ready, c.up("o"))
                for tt in range(TT):
                    ins = dve.tensor_scalar(O2[:, tt, cols(head * HD, HD)], tb[:, 2, tt * P:(tt + 1) * P], resum[:, tt:tt + 1],
                                            None, ALU.mult)
                ins.then_inc(tb_free[2], 1)

            split(8, 2 * HN)
            dve.wait_ge(tr_copy, c.at("copy"))
            turn_queries(0)
            with c.loop(dve, HEADS2 // 2 - 1, unit=16, s=2, exp=2, o=2, chain=10) as i:
                for e in range(2):
                    attention(i * 2 + e, 1 - e)
            attention(HEADS2 - 2, 1, ahead=UNIT)
            for i in range(4):
                if i == 0:
                    attention(HEADS2 - 1, now=UNIT, ahead=UNIT)
                else:
                    split(8)
                for tt in range(TT):
                    dve.wait_ge(acc_free[2 * (i % 2) + tt], (TILES_BEFORE_OUT_B - 4 + i) // 2 + 2)
                    ins = dve.tensor_tensor(tok[:, 0, tt, :], O2[:, tt, i * N:(i + 1) * N], sgt[:, tt, :], ALU.mult)
                ins.then_inc(tok_ready, 1)
                take_lo_tile(Hl, Hh, 4 * i)
            for i in range(4):
                split(8 if i < 3 else 4)
                tile_done(RING if i < 3 else 0)
                for tt in range(TT):
                    xt = x[:, tt, i * N:(i + 1) * N]
                    dve.tensor_tensor(xt, acc[:, 2 * (i % 2) + tt, :], xt, ALU.add).then_inc(acc_free[2 * (i % 2) + tt], 1)
            dve.wait_ge(evac, c.up("evac", 4))
            sum_squares()
            rms(D)
            dve.wait_ge(row_ready, 3 * 4)
            for tt in range(TT):
                for q in range(4):
                    xt = x[:, tt, q * N:(q + 1) * N]
                    ins = dve.scalar_tensor_tensor(xt, xt, rstd[:, tt:tt + 1], tb[:, q, :], ALU.mult, ALU.mult)
                ins.then_inc(out_ready, 1)

        @block.tensor
        def _(pe):
            c = Counts()
            pe.sem_inc(unit_used, RING)
            pe.sem_inc(mod_read, 2)
            for b in range(4):
                pe.sem_inc(acc_free[b], 1)
                pe.sem_inc(tb_free[b], 1)

            def products(dst, h, l, k, s, kts, n, first, last):
                for i in range(kts):
                    for tt in range(TT):
                        a, b = h[:, k + i, tt * P:(tt + 1) * P], l[:, k + i, tt * P:(tt + 1) * P]
                        w = slice(i * n, (i + 1) * n)
                        pe.matmul(dst(tt), a, hi[:, s, w], start=first and i == 0, stop=False)
                        pe.matmul(dst(tt), a, lo[:, s, w], start=False, stop=False)
                        mm = pe.matmul(dst(tt), b, hi[:, s, w], start=False, stop=last and i == kts - 1)
                mm.then_inc(unit_used, 1)

            def tile(h, l, pair, units, n=N, kts=2, k=0, dst=None, before={}, after={}):
                if dst is None:
                    for tt in range(TT):
                        pe.wait_ge(acc_free[2 * pair + tt], c.at(f"acc{pair}") + 1)
                    c.up(f"acc{pair}")
                    dst = lambda tt: acc[:, 2 * pair + tt, 0:n]
                for i in range(units):
                    if i in before:
                        before[i]()
                    s = c.slot("unit", RING)
                    pe.wait_ge(unit_split, c.up("unit") + START_UNITS)
                    products(dst, h, l, k + kts * i, s, kts, n, i == 0, i == units - 1)
                    if i in after:
                        after[i]()

            def read_out(pair):
                for tt in range(TT):
                    pe.wait_ge(acc_free[2 * pair + tt], c.at(f"acc{pair}") + 1)

            def taken(*banks):
                for b in banks:
                    pe.wait_ge(tb_free[b], c.at(f"tb{b}") + 1)

            def fill(b):
                taken(b)
                c.up(f"tb{b}")

            def transpose_pair(src, b, done):
                fill(b)
                for j in range(2):
                    for tt in range(TT):
                        ins = pe.transpose(tb[:, b, j * T + tt * P:j * T + (tt + 1) * P], src(tt, j), ident[:])
                ins.then_inc(done, 1)

            def transpose_tile(src, done):
                for b in range(2):
                    transpose_pair(lambda tt, j: src(tt)[:, (2 * b + j) * P:(2 * b + j + 1) * P], b, done)

            def transpose_tok(slot, done):
                transpose_tile(lambda tt: tok[:, slot, tt, :], done)

            def turned(slot, done=tr_copy):
                pe.wait_ge(tok_ready, c.up("tok"))
                transpose_tok(slot, done)

            def mod_sum(b, late=True):
                for q in range(4):
                    at = (c.at("late") + START_BLOCKS if late else c.at("start")) * 4 + q
                    ins = pe.matmul(tb[:, 3, cols(at, 1)], macc[:, b, q * P:(q + 1) * P], ones[:], start=True, stop=True)
                ins.then_inc(mod_read, 1)
                c.up("late" if late else "start")

            def late_sum(mods):
                pe.wait_ge(mod_taken, mods)
                b = c.slot("late", 2)
                pe.wait_ge(mod_done, (c.at("late") + 1) * MOD_UNITS)
                mod_sum(b)

            def spread(src, bank):
                for q in range(4):
                    b = bank(q)
                    fill(b)
                    for j in range(4):
                        ins = pe.matmul(tb[:, b, j * P:(j + 1) * P], src(4 * q + j).to_broadcast([P, P]), ident[:],
                                        start=True, stop=True)
                    ins.then_inc(row_ready, 1)

            pe.wait_ge(const_in, 7 * 16)
            pe.wait_ge(memory_set, 1)
            pe.wait_ge(xn_ready, TT)
            for k in range(KD // 2):
                transpose_pair(lambda tt, j: xn[:, tt, (2 * k + j) * P:(2 * k + j + 1) * P], k % 3, tr_copy)
            with c.loop(pe, START_BLOCKS // 2, start=2):
                for b in range(2):
                    pe.wait_ge(unit_split, (c.at("start") + 1) * MOD_UNITS)
                    mod_sum(b, late=False)
            tile(Hh, Hl, 0, 8, before={j: (lambda j=j: pe.wait_ge(in_split, j // 2 + 1)) for j in range(0, 8, 2)})
            tile(Hh, Hl, 1, 2, n=80, kts=8)
            read_out(0)
            transpose_tok(0, tr_split)

            def index_keys():
                pe.wait_ge(kidx_ready, 1)
                fill(2)
                for tt in range(TT):
                    ins = pe.transpose(tb[:, 2, tt * P:(tt + 1) * P], kd[:, tt, :], ident[:])
                ins.then_inc(tr_copy, 1)

            tile(Hh, Hl, 0, 8, after={7: index_keys})
            tile(Hh, Hl, 1, 8, after={1: lambda: turned(1), 5: lambda: late_sum(1)})
            for t in range(4):
                tile(qlath, qlatl, t % 2, 2, after={1: lambda: turned(t % 2)})

            def logits(q):
                if q == 0:
                    taken(0, 1, 2)
                if q >= 2:
                    pe.wait_ge(relu_ready, q - 1)
                b, w = q % 2, P if q % 2 == 0 else T
                pe.matmul(tb[:, b, 0:2 * w].rearrange("p (h s) -> p h s", h=2), qidxT[:, q // 2, b * P:(b + 1) * P],
                          kT2[:, :, 0:w], start=True, stop=True).then_inc(idx_ready, 1)

            def after_values(first, units=8):
                return {i: (lambda q=first + i: logits(q)) for i in range(units) if 0 <= first + i < IH}

            hooks = after_values(-2)
            hooks[1] = lambda: turned(0)
            tile(Hh, Hl, 0, 8, after=hooks)
            tile(Hh, Hl, 1, 8, after=after_values(6))
            hooks = after_values(14)
            hooks[2] = lambda: late_sum(1)
            tile(Hh, Hl, 0, 8, after=hooks)
            tile(Hh, Hl, 1, 8, after={7: lambda: late_sum(1)})

            def spatial(first):
                if first == 0:
                    pe.wait_ge(v_normed, 1)
                    pe.wait_ge(ws_ready, 1)
                    pe.wait_ge(relu_ready, IH)
                for g in range(first, first + 4):
                    b = g // 2 % 2
                    if g % 2 == 0:
                        fill(b)
                    ins = pe.matmul(tb[:, b, (g % 2) * T:(g % 2 + 1) * T].rearrange("p (t d) -> p t d", t=TT), wsT[:, g, :],
                                    z[:, :, g * P:(g + 1) * P], start=True, stop=True)
                    if g % 2 == 1:
                        ins.then_inc(gmlp_ready, 1)

            tile(Hh, Hl, 0, 8)
            tile(Hh, Hl, 1, 8, after={3: lambda: spatial(0), 7: lambda: spatial(4)})
            with c.loop(pe, HEADS1 // 2, unit=16, acc0=1, acc1=1, tb0=2, tb1=2, tb2=2, late=2, head=2, exp=2):
                for e in range(2):
                    head = c.at("head")

                    def scores():
                        pe.wait_ge(copied, c.up("head"))
                        fill(0)
                        pe.matmul(tb[:, 0, 0:T], qs[:, e, P:T], kT[:, cols(head, 1), :].rearrange("p a t -> p (a t)"),
                                  start=True, stop=True)
                        pe.matmul(tb[:, 0, T:T + P], qs[:, e, 0:P], kT[:, cols(head, 1), 0:P].rearrange("p a t -> p (a t)"),
                                  start=True, stop=True).then_inc(s_ready, 1)

                    def key_major():
                        pe.wait_ge(exp_ready, c.up("exp"))
                        fill(1)
                        for i in range(3):
                            ins = pe.transpose(tb[:, 1, i * P:(i + 1) * P], att1[:, i * P:(i + 1) * P], ident[:])
                        ins.then_inc(tr_copy, 1)

                    def output():
                        taken(1)
                        fill(2)
                        vh = lambda tt: v[:, tt, cols(head * HD, HD)]
                        pe.matmul(tb[:, 2, 0:HD], pt1[:, T:T + P], vh(0), start=True, stop=True)
                        pe.matmul(tb[:, 2, HD:2 * HD], pt1[:, 0:P], vh(0), start=True, stop=False)
                        pe.matmul(tb[:, 2, HD:2 * HD], pt1[:, P:T], vh(1), start=False, stop=True).then_inc(o_ready, 1)

                    tile(Hh, Hl, e, 8, after={1: scores, 3: lambda: late_sum(1), 4: key_major, 6: output})
            late_sum(1)
            taken(0, 1)
            for g in range(2):
                transpose_tile(lambda tt: z[:, tt, GW + g * N:GW + (g + 1) * N], tr_split)

            def attended(g):
                taken(2)
                transpose_tile(lambda tt: O1[:, tt, g * N:(g + 1) * N], tr_split)

            def spread_gate_m():
                pe.wait_ge(gate_ready, 1)
                spread(lambda j: fG[:, j:j + 1], lambda q: 2)

            def second_attended():
                attended(1)
                spread_gate_m()

            split_now = lambda: taken(0, 1)
            tile(Hh, Hl, 0, 4, before={0: split_now}, after={1: lambda: attended(0), 3: second_attended})
            tile(Hh, Hl, 1, 4, k=8, before={0: split_now})
            with c.loop(pe, 3, unit=8, acc0=1, acc1=1, tb0=1, tb1=1, tok=1):
                tile(Hh, Hl, 0, 4, after={1: lambda: turned(0, tr_split)})
                tile(Hh, Hl, 1, 4, k=8)
            for t in range(4):
                if t == 0:
                    tile(mergedh, mergedl, 0, 8, before={6: split_now}, after={1: lambda: turned(0, tr_split)})
                else:
                    tile(mergedh, mergedl, t % 2, 8, after={3: lambda: late_sum(2)})
            late_sum(2)
            pe.wait_ge(mod_taken, 3)
            pe.wait_ge(xn_ready, 2 * TT)
            split_by = []
            for k in range(KD // 2):
                transpose_pair(lambda tt, j: mix[:, tt, (2 * k + j) * P:(2 * k + j + 1) * P], k % 4, tr_split)
                split_by.append((tb_free[k % 4], c.at(f"tb{k % 4}") + 1))

            def when_split(units):
                return {j: (lambda j=j: pe.wait_ge(*units[j])) for j in range(8)}

            def next_hidden():
                def hidden():
                    read_out(1)
                    transpose_tok(0, tr_split)

                tile(Hh, Hl, 0, 8, after={1: hidden})
                tile(Hh, Hl, 1, 8)

            tile(Hh, Hl, 0, 8, before=when_split(split_by))
            tile(Hh, Hl, 1, 8)
            with c.loop(pe, FT - 1, unit=16, acc0=1, acc1=1, tb0=1, tb1=1):
                next_hidden()

            def last_hidden():
                read_out(1)
                transpose_tok(0, tr_split)
                pe.wait_ge(gate_ready, 2)
                spread(lambda j: fG[:, j:j + 1], lambda q: 2)

            for t in range(4):
                if t == 0:
                    tile(hidh, hidl, 0, FK // 2, before={FK // 2 - 2: split_now}, after={1: last_hidden})
                else:
                    tile(hidh, hidl, t % 2, FK // 2)
            pe.wait_ge(x_ready, 2 * TT)
            split_by = []
            for k in range(KD // 2):
                transpose_pair(lambda tt, j: x[:, tt, (2 * k + j) * P:(2 * k + j + 1) * P], k % 4, tr_split)
                split_by.append((tb_free[k % 4], c.at(f"tb{k % 4}") + 1))
            pe.wait_ge(pool_loaded, 16)

            def pooling_group(g, before={}, after={}):
                def pooled():
                    read_out(0)
                    for b in range(2):
                        fill(2 + b)
                        for j in range(2):
                            us = lambda s: u[:, s, (2 * b + j) * P:(2 * b + j + 1) * P]
                            m = lambda at, n: poolM[:, cols(g, 1), at:at + n].rearrange("p a t -> p (a t)")
                            at = j * T
                            pe.matmul(tb[:, 2 + b, at:at + T], us(0), m(0, T), start=True, stop=False)
                            ins = pe.matmul(tb[:, 2 + b, at + P:at + T], us(1), m(T, P), start=False, stop=True)
                        ins.then_inc(tr_split, 1)

                def group_banks():
                    fill(2)
                    fill(3)

                tile(Hh, Hl, 0, 8, before=before, after=after)
                tile(Hh, Hl, 1, 8, after={1: pooled})
                tile(ph, pl, None, 4, kts=1, dst=lambda tt: tb[:, 2 + tt, :], before={0: group_banks})

            def last_group():
                taken(2, 3)
                transpose_tok(1, tr_split)

            pooling_group(0, before=when_split(split_by))
            with c.loop(pe, 3, unit=20, acc0=1, acc1=1, tb0=1, tb1=1, tb2=2, tb3=2) as g:
                pooling_group(g + 1, after={1: last_group})
            with c.loop(pe, 2, unit=16, acc0=1, acc1=1, tb0=2, tb1=2):
                for e in range(2):
                    def last_tile():
                        taken(2, 3)
                        read_out(1 - e)
                        transpose_tok(1 - e, tr_split)

                    tile(zh, zl, e, 8, before={6: split_now}, after={1: last_tile})
            def last_out():
                read_out(1)
                transpose_tok(1, tr_split)

            tile(Hh, Hl, 0, 8, before={6: split_now}, after={1: last_out})
            tile(Hh, Hl, 1, 8, after={1: lambda: turned(0)})
            with c.loop(pe, 3, unit=16, acc0=1, acc1=1, tb0=1, tb1=1, tok=1):
                tile(Hh, Hl, 0, 8)
                tile(Hh, Hl, 1, 8, after={1: lambda: turned(0)})

            def attention(head):
                def turned_queries():
                    pe.wait_ge(tok_ready, c.up("tok"))
                    for b, gs in ((0, (0, 1)), (1, (2,))):
                        fill(b)
                        for g in gs:
                            for tt in range(TT):
                                ins = pe.transpose(tb[:, b, (g % 2) * T + tt * P:(g % 2) * T + (tt + 1) * P],
                                                   tok[:, 0, tt, g * P:(g + 1) * P], ident[:])
                        ins.then_inc(tr_copy, 1)

                def scores():
                    k = lambda n: k2T[:, cols(head, 1), 0:n].rearrange("p a t -> p (a t)")
                    fill(0)
                    fill(1)
                    for g in range(NG):
                        pe.matmul(tb[:, g // 2, (g % 2) * T:(g % 2 + 1) * T], qTh[:, g, P:T], k(T), start=True, stop=True)
                    fill(2)
                    for g in range(NG):
                        ins = pe.matmul(tb[:, 2, g * P:(g + 1) * P], qTh[:, g, 0:P], k(P), start=True, stop=True)
                    ins.then_inc(s_ready, 1)

                def key_major():
                    pe.wait_ge(p_ready, c.up("p"))
                    fill(3)
                    S1 = NG * T
                    for i, at in enumerate((0, P, S1)):
                        ins = pe.transpose(tb[:, 3, i * P:(i + 1) * P], att2[:, at:at + P], ident[:])
                    ins.then_inc(tr_copy, 1)

                def output():
                    taken(3)
                    fill(2)
                    vh = lambda tt: v2[:, tt, cols(head * HD, HD)]
                    pe.matmul(tb[:, 2, 0:HD], pt2[:, T:T + P], vh(0), start=True, stop=True)
                    pe.matmul(tb[:, 2, HD:2 * HD], pt2[:, 0:P], vh(0), start=True, stop=False)
                    pe.matmul(tb[:, 2, HD:2 * HD], pt2[:, P:T], vh(1), start=False, stop=True).then_inc(o_ready, 1)

                return {1: turned_queries, 3: scores, 6: key_major, 7: output}

            tile(hbh, hbl, 0, 8, n=HN)
            with c.loop(pe, HEADS2 // 2 - 1, unit=16, acc0=1, acc1=1, tb0=4, tb1=4, tb2=4, tb3=2, tok=2, p=2) as i:
                for e in range(2):
                    tile(hbh, hbl, 1 - e, 8, n=HN, after=attention(i * 2 + e))
            tile(hbh, hbl, 1, 8, n=HN, after=attention(HEADS2 - 2))
            tile(hbh, hbl, 0, 8, after=attention(HEADS2 - 1))
            for t in range(1, 4):
                tile(hbh, hbl, t % 2, 8, after={1: lambda: turned(0, tr_split)})
            for t in range(4):
                if t == 0:
                    tile(Hh, Hl, 0, 8, before={6: split_now}, after={1: lambda: turned(0, tr_split)})
                else:
                    tile(Hh, Hl, t % 2, 8)
            spread(lambda j: vec("norm_f", j), lambda q: q)


def _units(w, kts=2):
    k, n = w.shape
    return w.reshape(k // (kts * P), kts, P, n // N, N).transpose(3, 0, 2, 1, 4).reshape(-1, P, kts * N)


def _fm(v):
    return v.reshape(-1, P).T


def _rope(dim):
    inv = 1.0 / (np.float32(10000.0) ** (np.arange(0, dim, 2, dtype=np.float32) / np.float32(dim)))
    ang = np.arange(T, dtype=np.float32)[:, None] * inv[None, :].astype(np.float32)
    cos, sin = np.cos(ang), np.sin(ang)
    lay = lambda a: a.reshape(TT, P, dim).transpose(1, 0, 2).reshape(P, TT * dim)
    return lay(np.concatenate([cos, cos], 1)), lay(np.concatenate([-sin, sin], 1))


def _constants():
    table = np.concatenate([np.eye(P), *_rope(HD), *_rope(IROPE)], 1).astype(np.float32)
    t, s = np.arange(T)[:, None], np.arange(T)[None, :]
    mask1 = np.where(s <= t, 0, -BIG)[:P, :P].astype(np.float32)
    mask2 = np.stack([np.where((s <= t) & (t - s <= window) & ((t - s) % d == 0), 0, -BIG)[P:]
                      for window, d in ((128, 1), (512, 4), (2048, 16))], 1).astype(np.float32)
    pool = []
    for window in (2, 4, 8, 16):
        m = np.where((s <= t) & (s > t - window), 1.0 / np.minimum(t + 1, window), 0.0) - np.eye(T)
        pool.append(np.concatenate([m.T[:P], m.T[P:, P:]], 1))
    return table, mask1, mask2, np.stack(pool, 1).astype(np.float32)


def _layout(a):
    w_mod, b_mod = a["w_mod"][0], a["b_mod"][0]
    w_in, w_in_a, w_in_b = a["w_in"][0], a["w_in_a_2"][0], a["w_in_b_2"][0]
    shift_m, scale_m, gate_m, shift_f, scale_f, gate_f = range(6)
    blocks = [m * D + b * N for b in range(4) for m in (scale_m, shift_m)]
    blocks += [m * D + b * N for m in (gate_m, scale_f, shift_f, gate_f) for b in range(4)]
    wmod = [_units(w_mod[:, at:at + N]) for at in blocks]
    b_mod = np.concatenate([b_mod[at:at + N] for at in blocks])

    fm = np.concatenate([_fm(v) for v in (
        a["c"][0], b_mod, a["g_pre_mix"][0], a["g_post_mix"][0], a["q_lat_norm_g"][0], a["g_pre_ffn"][0],
        a["g_post_ffn"][0], a["norm_a_2"][0], a["scale_a_2"][0], a["norm_kv_2"], a["norm_b_2"][0], a["norm_f_2"],
        a["gmlp_b_s"][0].reshape(-1))], 1)
    assert fm.shape == (P, FM_COLS)

    at_q, at_k = 2 * GW, 2 * GW + QLAT
    at_v = at_k + GW
    at_i = at_v + GW
    at_g = at_i + IDIM + IH
    kidx = np.zeros((2, P, UNIT), np.float32)
    kidx[:, :, 0:640] = w_in[:, at_i:at_g].reshape(2, 8, P, 80).transpose(0, 2, 1, 3).reshape(2, P, 640)
    wa = [_units(w_in[:, at_q:at_k]), kidx, _units(w_in[:, at_k:at_v]), _units(a["w_qidx_up"][0]), _units(a["w_q_up"][0]),
          _units(w_in[:, at_v:at_i]), _units(w_in[:, GW:at_q]), _units(w_in[:, 0:GW]), _units(w_in[:, at_g:])]

    def by_tile(*ws):
        return [_units(w[:, n:n + N]) for n in range(0, ws[0].shape[1], N) for w in ws]

    wa += by_tile(a["w_proj_a"][0], a["w_proj_b"][0])
    wa += [_units(a["w_out"][0])]
    wa += by_tile(a["w_ffn_gate"][0], a["w_ffn_up"][0])
    wa += [_units(a["w_ffn_down"][0])]
    for g in range(4):
        grp = np.zeros((4, P, UNIT), np.float32)
        grp[:, :, 0:N] = a["w_grp_a_2"][0, g].reshape(4, P, N)
        wa += [_units(w_in_a[:, g * N:(g + 1) * N]), _units(w_in_a[:, D + g * N:D + (g + 1) * N]), grp]
    wa += [_units(a["w_out_a_2"][0])]
    wa += by_tile(a["w_k_2"], a["w_v_2"])
    wq = w_in_b[:, 0:NG * D].reshape(KD // 2, 2, P, NG, HEADS2, HD).transpose(4, 0, 2, 1, 3, 5)
    wc = [_units(w_in_b[:, NG * D:]), _units(a["w_out_b_2"][0])]

    table, mask1, mask2, pool = _constants()
    kidx_gb = np.broadcast_to(np.stack([a["kidx_ln_g"][0], a["kidx_ln_b"][0]]), (P, 2, IDIM))
    arrays = [a["x"][0].reshape(TT, P, D).transpose(1, 0, 2), fm, np.stack([a["gmlp_ln_g"][0], a["gmlp_ln_b"][0]]), table,
              mask1, mask2, pool, a["gmlp_w_s"][0].transpose(2, 0, 1), kidx_gb,
              np.concatenate(wmod[:START_BLOCKS]), np.concatenate(wmod[START_BLOCKS:]),
              np.concatenate(wa), wq.reshape(B_UNITS, P, 2 * HN), np.concatenate(wc)]
    assert arrays[-3].shape[0] == A_UNITS and arrays[-1].shape[0] == C_UNITS
    return [np.ascontiguousarray(v) for v in arrays]


_INS = ["x", "fm", "row", "table", "mask1", "mask2", "pool", "ws", "kidx", "wmod0", "wmod1", "wa", "wb", "wc"]


def kernel(**inputs):
    import concourse.bacc as bacc
    from concourse.bass_utils import run_bass_kernel_spmd

    nc = bacc.Bacc("TRN2", target_bir_lowering=False, num_devices=1)
    arrays, args = {}, []
    for name, v in zip(_INS, _layout({k: np.asarray(v) for k, v in inputs.items()})):
        arrays[f"in_{name}_dram"] = v
        args.append(nc.dram_tensor(f"in_{name}_dram", v.shape, mybir.dt.from_np(v.dtype), kind="ExternalInput").ap())
    out = nc.dram_tensor("out_0_dram", (1, T, D), F32, kind="ExternalOutput").ap()
    two_blocks(nc, *args, out[0])
    r = run_bass_kernel_spmd(nc, [arrays], core_ids=[0])
    return r.results[0]["out_0_dram"]
```

```python
from contextlib import ExitStack, contextmanager

import numpy as np

import concourse.bass as bass
from concourse import mybir

F32 = mybir.dt.float32
F32R = mybir.dt.float32r
BF16 = mybir.dt.bfloat16
ALU = mybir.AluOpType
ACT = mybir.ActivationFunctionType
AX_X = mybir.AxisListType.X

P = 128
TT = 2
T = TT * P
D = 2048
KD = D // P
N = 512
UNIT = 1024
RING = 4
GW = 1024
HEADS1, HEADS2, HD = 8, 16, 128
QLAT = 512
IH, IDIM, IROPE = 16, 64, 32
TOPK = 64
FFN = 5632
FT = FFN // N
FK = FFN // P
NG = 3
HN = NG * HD
EPS = 1e-6
SCALE = HD ** -0.5
IDX_SCALE = IH ** -0.5 * IDIM ** -0.5
BIG = 1e30
TAKEN = -3e38

START_BLOCKS = 8
LATE_BLOCKS = 16
MOD_UNITS = KD // 2

FM, FM_COLS = {}, 0
for _name, _cols in (("c", KD), ("b_mod", 96), ("g_pre_mix", KD), ("g_post_mix", KD), ("qlat_g", 4),
                     ("g_pre_ffn", KD), ("g_post_ffn", KD), ("norm_a", KD), ("scale_a", KD),
                     ("norm_kv", KD), ("norm_b", KD), ("norm_f", KD), ("b_s", 8)):
    FM[_name] = FM_COLS
    FM_COLS += _cols
GATE_M, SCALE_F, SHIFT_F, GATE_F = (4 * (START_BLOCKS + 4 * i) for i in range(4))

A_UNITS = 8 + 2 + 2 * 8 + 4 + 4 + 2 * 8 + 4 * 8 + 8 * 8 + 4 * 8 + 4 * 8 + FT * 16 + 4 * (FK // 2) + 4 * 20 + 3 * 32
B_UNITS = HEADS2 * 8
C_UNITS = 64
START_UNITS = START_BLOCKS * MOD_UNITS
QUARTERS, QUARTER_MOD, QUARTER_W = 4, 2 * MOD_UNITS, 4
QUARTER = QUARTER_MOD + QUARTER_W
assert MOD_UNITS % RING == 0 and QUARTER_W % RING == 0


def units_to_block(block):
    return MOD_UNITS * (block + 1) + QUARTER_W * ((block - 1) // 2 if block else 0)


UV0, GATES0, MERGE0, OUT0, FFN0 = 50, 82, 146, 178, 210
FFN_MOD = 4
_looped = [at + i for at in [GATES0 + 16 * t for t in range(HEADS1 // 2)] + [FFN0 + 16 * t for t in range(FFN_MOD)]
           for i in range(7, 7 + MOD_UNITS)]
LATE = sorted([UV0 + i for at in (0, 12, 24) for i in range(at, at + MOD_UNITS)] + _looped +
              [MERGE0 + i for i in (8, 9, 10, 11, 16, 17, 18, 19, 24, 25, 26, 27)] + list(range(OUT0, OUT0 + 28)))
LOOPED = [b for b in range(LATE_BLOCKS) if LATE[b * MOD_UNITS] in _looped]
assert len(LATE) == len(set(LATE)) == LATE_BLOCKS * MOD_UNITS
MODS = {0: QUARTER_MOD + MOD_UNITS, QUARTER_W: QUARTER_MOD, 2 * QUARTER_W: QUARTER_MOD, 3 * QUARTER_W: MOD_UNITS}
MODS.update({unit: 1 for unit in LATE})
LATE_SUMS = [UV0 + 7, UV0 + 19] + [GATES0 + 2 + 16 * t for t in range(HEADS1 // 2)] + [MERGE0 + 1, MERGE0 + 23] + \
    [OUT0 + 4 + 8 * t for t in range(4)] + [FFN0 + 19 + 16 * t for t in range(FFN_MOD)]
TAKES = [unit + 5 for unit in LATE_SUMS]
assert all(LATE[b * MOD_UNITS + MOD_UNITS - 1] <= unit for b, unit in enumerate(LATE_SUMS))
STREAM = START_UNITS + LATE_BLOCKS * MOD_UNITS + A_UNITS

TILES_BEFORE_MERGE = 10 + 4 + 8
TILES_BEFORE_OUT_A = TILES_BEFORE_MERGE + 8 + 4 + 2 * FT + 4 + 8
TILES_BEFORE_OUT_B = TILES_BEFORE_OUT_A + 4 + 8 + HEADS2 + 4
K_COPIED = KD // 2 + 1 + 2
COPIES_BEFORE_K2 = K_COPIED + 2 + 8 + HEADS1


class Counts:

    def __init__(self):
        self.n, self.turn, self.steps = {}, None, {}

    def at(self, name, div=1):
        n = self.n.get(name, 0) // div
        step = self.steps.get(name, 0)
        if self.turn is None or not step:
            return n
        assert step % div == 0
        return self.turn * (step // div) + n

    def up(self, name, k=1, div=1):
        self.n[name] = self.n.get(name, 0) + k
        return self.at(name, div)

    def slot(self, name, ring):
        assert self.turn is None or self.steps.get(name, 0) % ring == 0, name
        return self.n.get(name, 0) % ring

    @contextmanager
    def loop(self, engine, turns, **steps):
        first = dict(self.n)
        self.steps = steps
        with engine.Fori(0, turns) as turn:
            self.turn = turn
            yield turn
        self.turn, self.steps = None, {}
        done = {k: v - first.get(k, 0) for k, v in self.n.items() if v != first.get(k, 0)}
        assert done == steps, (done, steps)
        for k, s in steps.items():
            self.n[k] = first.get(k, 0) + turns * s


def two_blocks(nc, x_in, fm_in, row_in, table_in, mask1_in, mask2_in, pool_in, ws_in, kidx_in,
               wa, wb, wc, out):
    with ExitStack() as ctx:
        def sem(name):
            return ctx.enter_context(nc.semaphore(name))

        top = [nc.sbuf_base + 127 & ~127]

        def sb(name, shape, dt=F32, at=None):
            size = int(np.prod(shape[1:])) * (2 if dt == BF16 else 4)
            if at is None:
                at = top[0] + 31 & ~31
                top[0] = at + size
            return nc.alloc_sbuf_tensor_at(name, shape, dt, offset=at)

        raw = sb("raw", [P, RING, UNIT])
        hi = sb("hi", [P, RING, UNIT], F32R)
        lo = sb("lo", [P, RING, UNIT], F32R)
        x_at = top[0]
        x = sb("x", [P, TT, D])
        tok_at = top[0]
        tok = sb("tok", [P, 2, TT, N])
        junk_x = sb("junk_x", [P, TT, D], BF16, at=tok_at)
        junk = sb("junk", [P, TT, N], BF16)
        ident = sb("ident", [P, P])
        fm = sb("fm", [P, FM_COLS])
        modfm = sb("modfm", [P, 96])
        fA = sb("fA", [P, KD])
        fG = sb("fG", [P, KD])
        ropeC = sb("ropeC", [P, TT, HD])
        ropeS = sb("ropeS", [P, TT, HD])
        iropeC = sb("iropeC", [P, TT, IROPE])
        iropeS = sb("iropeS", [P, TT, IROPE])
        ones = sb("ones", [P, 1])
        ssq = sb("ssq", [P, TT])
        ssqp = sb("ssqp", [P, TT, 4])
        var = sb("var", [P, TT])
        std = sb("std", [P, TT])
        rstd = sb("rstd", [P, TT])
        stats = sb("stats", [P, TT, 2, 6])
        mv = sb("mv", [P, TT, 2])
        nmax = sb("nmax", [P, TT])
        esum = sb("esum", [P, TT])
        resum = sb("resum", [P, TT])
        best8 = sb("best8", [P, TT, 8])
        sgt = sb("sgt", [P, TT, N])
        h_at = top[0]
        Hh = sb("Hh", [P, KD, T], F32R)
        Hl = sb("Hl", [P, KD, T], F32R)
        free = top[0]
        KB = 1024
        kT = sb("kT", [P, HEADS1, T], at=free)
        macc0 = sb("macc0", [P, 2, 2, N], at=free)
        v = sb("v", [P, TT, GW], at=free + 8 * KB)
        qT = sb("qT", [P, HEADS1, T], at=free + 16 * KB)
        qidxT = sb("qidxT", [P, IH // 2, T], at=free + 24 * KB)
        O1 = sb("O1", [P, TT, GW], at=free + 24 * KB)
        mergedh = sb("mergedh", [P, KD, T], F32R, at=free)
        mergedl = sb("mergedl", [P, KD, T], F32R, at=free + 16 * KB)
        sg_at = free + 32 * KB
        sg = sb("sg", [P, TT, 2 * D], at=sg_at)
        xn = sb("xn", [P, TT, D], at=sg_at)
        wsT = sb("wsT", [P, 8, P], at=sg_at)
        kT2 = sb("kT2", [P, 2, T], at=sg_at + 4 * KB)
        kn = sb("kn", [P, TT, IDIM], at=sg_at + 6 * KB)
        kr = sb("kr", [P, TT, IROPE], at=sg_at + 6 * KB + 512)
        kidx_gb = sb("kidx_gb", [P, 2, IDIM], at=sg_at + 6 * KB + 768)
        xnT = sb("xnT", [P, KD, T], at=sg_at + 16 * KB)
        ln_g = sb("ln_g", [P, GW], at=sg_at + 24 * KB)
        ln_b = sb("ln_b", [P, GW], at=sg_at + 28 * KB)
        mix = sb("mix", [P, TT, D], at=sg_at)
        q_at = sg_at + 32 * KB
        qlath = sb("qlath", [P, 4, T], F32R, at=q_at)
        qlatl = sb("qlatl", [P, 4, T], F32R, at=q_at + 4 * KB)
        gm1 = sb("gm1", [P, D], at=q_at)
        top[0] = q_at
        score = sb("score", [P, 384])
        work = sb("work", [P, 384])
        top[0] = q_at + 8 * KB
        rl = sb("rl", [P, 2, 512])
        top[0] -= 4 * KB
        kd = sb("kd", [P, TT, P])
        top[0] -= KB
        att1 = sb("att1", [P, 384])
        pt1 = sb("pt1", [P, 384])
        top[0] = q_at + 12 * KB
        selb = sb("selb", [P, 384])
        kx = sb("kx", [P, TT, 80])
        qs = sb("qs", [P, 2, T])
        mask1 = sb("mask1", [P, P])
        macc = sb("macc", [P, 2, N])
        macc_ffn = sb("macc_ffn", [P, N], at=tok_at + TT * N * 4)
        end1 = top[0]
        z = sb("z", [P, TT, D], at=x_at)
        hidh = sb("hidh", [P, FK, T], F32R, at=free)
        hidl = sb("hidl", [P, FK, T], F32R, at=free + FK * T * 4)
        fmix = sb("fmix", [P, TT, D], at=h_at)
        gm2 = sb("gm2", [P, D], at=h_at + 16 * KB)
        zh = sb("zh", [P, KD, T], F32R, at=free)
        zl = sb("zl", [P, KD, T], F32R, at=free + 16 * KB)
        hbh = sb("hbh", [P, KD, T], F32R, at=free + 32 * KB)
        hbl = sb("hbl", [P, KD, T], F32R, at=free + 48 * KB)
        top[0] = free + 64 * KB
        u = sb("u", [P, TT, N])
        ph = sb("ph", [P, 4, T], F32R)
        pl = sb("pl", [P, 4, T], F32R)
        poolM = sb("poolM", [P, 4, 384])
        k2T = sb("k2T", [P, HEADS2, T], at=free)
        v2 = sb("v2", [P, TT, D], at=free + 16 * KB)
        top[0] = free + 64 * KB
        O2 = sb("O2", [P, TT, D])
        top[0] = max(top[0], free + 64 * KB + 4 * KB + 8 * KB + 6 * KB)
        mask2 = sb("mask2", [P, NG, T])
        qTh = sb("qTh", [P, NG, T])
        att2 = sb("att2", [P, NG * 384])
        pt2 = sb("pt2", [P, 384], at=tok_at + TT * N * 4)
        assert max(end1, top[0], free + 2 * FK * T * 4) <= nc.sbuf_usable_end, (
            end1, top[0], free + 2 * FK * T * 4, nc.sbuf_usable_end)

        acc = ctx.enter_context(nc.psum_tensor("acc", [P, 4, N], F32))
        tb = ctx.enter_context(nc.psum_tensor("tb", [P, 4, N], F32))

        const_in = sem("const_in")
        fm_loaded = sem("fm_loaded")
        x_loaded = sem("x_loaded")
        row_loaded = sem("row_loaded")
        pool_loaded = sem("pool_loaded")
        mask_loaded = sem("mask_loaded")
        raw_loaded = [sem(f"raw_loaded{i}") for i in range(RING)]
        memory_set = sem("memory_set")
        ws_ready = sem("ws_ready")
        unit_split = sem("unit_split")
        hi_ready = sem("hi_ready")
        unit_used = sem("unit_used")
        acc_free = [sem(f"acc_free{i}") for i in range(4)]
        tb_free = [sem(f"tb_free{i}") for i in range(4)]
        tok_ready = sem("tok_ready")
        tr_split = sem("tr_split")
        tr_hi = sem("tr_hi")
        tr_copy = sem("tr_copy")
        copied = sem("copied")
        in_split = sem("in_split")
        in_scaled = sem("in_scaled")
        in_hi = sem("in_hi")
        var_ready = sem("var_ready")
        std_ready = sem("std_ready")
        ssq_ready = sem("ssq_ready")
        rstd_ready = sem("rstd_ready")
        evac = sem("evac")
        mod_read = sem("mod_read")
        mod_taken = sem("mod_taken")
        gate_ready = sem("gate_ready")
        row_ready = sem("row_ready")
        row_copied = sem("row_copied")
        kidx_ready = sem("kidx_ready")
        kidx_spread = sem("kidx_spread")
        idx_ready = sem("idx_ready")
        relu_ready = sem("relu_ready")
        relu_read = sem("relu_read")
        s_ready = sem("s_ready")
        att_ready = sem("att_ready")
        exp_ready = sem("exp_ready")
        p_ready = sem("p_ready")
        o_ready = sem("o_ready")
        gmlp_ready = sem("gmlp_ready")
        v_normed = sem("v_normed")
        y_ready = sem("y_ready")
        x_ready = sem("x_ready")
        xn_ready = sem("xn_ready")
        fa_ready = sem("fa_ready")
        out_ready = sem("out_ready")
        dve_chain = sem("dve_chain")
        stored = sem("stored")

        def cols(start, n):
            return bass.ds(start, n) if not isinstance(start, int) else slice(start, start + n)

        def vec(name, k, n=1):
            return fm[:, cols(k + FM[name], n)]

        def late_sums(block):
            if block in LOOPED:
                return macc[:, 0, :] if block < 8 else macc_ffn[:]
            return macc[:, block % 2, :]

        block = ctx.enter_context(nc.Block())

        @block.sync
        def _(sp):
            sp.dma_start(fm[:], fm_in).then_inc(fm_loaded, 16)
            c = Counts()

            def load(src):
                s = c.slot("unit", RING)
                if c.n.get("unit", 0) >= RING:
                    sp.wait_ge(unit_split, c.at("unit") - (RING - 1))
                sp.dma_start(raw[:, s, 0:src.shape[-1]], src).then_inc(raw_loaded[s], 16)
                c.up("unit")

            def stream(w, units):
                first = RING if not c.n.get("unit", 0) else 0
                for i in range(first):
                    load(w[i])
                turns = (units - first) // RING
                with c.loop(sp, turns, unit=RING) as turn:
                    for j in range(RING):
                        load(w[bass.ds(turn * RING + (first + j), 1)].rearrange("a p n -> (a p) n"))
                for i in range(first + turns * RING, units):
                    load(w[i])

            stream(wa, STREAM)
            stream(wb, B_UNITS)
            stream(wc, C_UNITS)
            for i in range(4 * TT):
                tt, n = i // 4, slice(i % 4 * N, (i % 4 + 1) * N)
                sp.wait_ge(out_ready, i + 1)
                sp.dma_start(out[tt * P:(tt + 1) * P, n], x[:, tt, n]).then_inc(stored, 16)
            sp.wait_ge(stored, 4 * TT * 16)

        @block.gpsimd
        def _(pool):
            pool.memset(ones[:], 1.0).then_inc(memory_set, 1)
            pool.wait_ge(row_loaded, 4 * 16)
            pool.memset(kT2[:], 0.0).then_inc(memory_set, 1)
            pool.affine_select(out=wsT[:], in_=wsT[:], compare_op=ALU.is_ge, fill=0.0, base=0,
                               pattern=[[0, 8], [1, P]], channel_multiplier=-1).then_inc(ws_ready, 1)

        @block.scalar
        def _(act):
            c = Counts()

            def split(units, n=UNIT):
                for _ in range(units):
                    c.up("raw", MODS.get(c.n.get("unit", 0), 0))
                    r, s = c.slot("raw", RING), c.slot("unit", RING)
                    act.wait_ge(raw_loaded[r], c.at("raw", RING) * 16 + 16)
                    c.up("raw")
                    act.wait_ge(unit_used, c.at("unit") + 1)
                    act.activation(hi[:, s, 0:n], raw[:, r, 0:n], ACT.Copy).then_inc(hi_ready, 1)
                    c.up("unit")

            def split_to(unit, n=UNIT):
                split(unit - c.n["unit"], n)

            def tile_done(ahead=RING):
                act.wait_ge(unit_used, c.at("unit") + (RING - ahead))

            def root():
                act.wait_ge(var_ready, c.up("var"))
                act.activation(std[:], var[:], ACT.Sqrt).then_inc(std_ready, 1)

            def take_hi(dst, k, b, gain=None, last=True):
                if gain is None:
                    ins = act.activation(dst[:, cols(k, 2), :], tb[:, b, :].rearrange("p (k t) -> p k t", k=2), ACT.Copy)
                else:
                    for j in range(2):
                        ins = act.activation(dst[:, cols(k + j, 1), :], tb[:, b:b + 1, j * T:(j + 1) * T], ACT.Copy,
                                             scale=gain(j))
                if last:
                    ins.then_inc(tr_hi, 1)

            def take_hi_tile(dst, k, gain=None):
                for b in range(2):
                    act.wait_ge(tr_split, c.up("split"))
                    take_hi(dst, k + 2 * b, b, gain and (lambda j, b=b: gain(2 * b + j)))

            def copy_tile(dst, k):
                for b in range(2):
                    act.wait_ge(tr_copy, c.up("copy"))
                    act.activation(dst[:, cols(k + 2 * b, 2), :], tb[:, b, :].rearrange("p (k t) -> p k t", k=2),
                                   ACT.Copy).then_inc(tb_free[b], 1)

            def read_out(dst_of, pair, func=ACT.Copy, scaled=False):
                for tt in range(TT):
                    ins = act.activation(dst_of(tt), acc[:, 2 * pair + tt, :], func,
                                         scale=rstd[:, tt:tt + 1] if scaled else 1.0)
                    ins.then_inc(acc_free[2 * pair + tt], 1)

            def square_tile(pair, col):
                tile_done(3)
                for tt in range(TT):
                    act.activation(junk[:, tt, :], acc[:, 2 * pair + tt, :], ACT.Square,
                                   accum_out=ssqp[:, tt, cols(col, 1)]).then_inc(evac, 1)

            def spread_rows(dst, banks=(2, 2, 2, 2)):
                for q, b in enumerate(banks):
                    act.wait_ge(row_ready, c.up("row"))
                    act.activation(dst[:, q * N:(q + 1) * N], tb[:, b, :], ACT.Copy).then_inc(tb_free[b], 1)

            def square_x():
                for i in range(2):
                    n = slice(i * D // 2, (i + 1) * D // 2)
                    for tt in range(TT):
                        act.wait_ge(x_ready, c.up("x"))
                        ins = act.activation(junk_x[:, tt, n], x[:, tt, n], ACT.Square, accum_out=ssqp[:, tt, i:i + 1])
                ins.then_inc(ssq_ready, 1)

            act.wait_ge(raw_loaded[RING - 1], 16)
            act.dma_start(x[:], x_in).then_inc(x_loaded, 16)
            act.dma_start(ident[:], table_in[:, 0:P]).then_inc(const_in, 16)
            at = P
            for dst, n in ((ropeC, TT * HD), (ropeS, TT * HD), (iropeC, TT * IROPE), (iropeS, TT * IROPE)):
                act.dma_start(dst[:], table_in[:, at:at + n].rearrange("p (a b) -> p a b", a=TT)).then_inc(const_in, 16)
                at += n
            act.dma_start(mask1[:], mask1_in).then_inc(const_in, 16)
            act.wait_ge(x_loaded, 16)
            for tt in range(TT):
                ins = act.activation(xn[:, tt, :], x[:, tt, :], ACT.Square, accum_out=ssq[:, tt:tt + 1])
            ins.then_inc(ssq_ready, 1)
            root()
            for k in range(KD // 2):
                act.wait_ge(tr_copy, c.up("copy"))
                act.activation(xnT[:, 2 * k:2 * k + 2, :], tb[:, k % 3, :].rearrange("p (k t) -> p k t", k=2), ACT.Copy)\
                    .then_inc(tb_free[k % 3], 1)
            for b in range(3):
                act.wait_ge(tb_free[b], 1 + len(range(b, KD // 2, 3)))
            for q in range(QUARTERS):
                split(QUARTER_W)
                act.wait_ge(fa_ready, q + 1)
                for k in range(4 * q, 4 * q + 4):
                    shift = 8 * q + 4 + k % 4
                    ins = act.activation(xnT[:, k, :], xnT[:, k, :], ACT.Identity, scale=fA[:, k:k + 1],
                                         bias=modfm[:, shift:shift + 1])
                ins.then_inc(in_scaled, 1)
                act.wait_ge(in_scaled, q + 1)
                act.activation(Hh[:, 4 * q:4 * q + 4, :], xnT[:, 4 * q:4 * q + 4, :], ACT.Copy).then_inc(in_hi, 1)
            act.wait_ge(in_split, 4)
            act.dma_start(wsT[:], ws_in).then_inc(row_loaded, 16)
            act.dma_start(kidx_gb[:], kidx_in).then_inc(row_loaded, 16)
            for i, row in enumerate((ln_g, ln_b)):
                act.dma_start(row[:], row_in[i].partition_broadcast(P))\
                    .then_inc(row_loaded, 16)

            split_to(18, 640)
            tile_done()
            for tt in range(TT):
                ins = act.activation(junk[:, tt, :], acc[:, tt, :], ACT.Square, accum_out=ssq[:, tt:tt + 1])
            ins.then_inc(ssq_ready, 1)
            root()
            split_to(20)
            take_hi_tile(qlath, 0, lambda j: vec("qlat_g", j))
            split_to(22)
            tile_done()
            for tt in range(TT):
                act.activation(kx[:, tt, :], acc[:, tt, 0:80], ACT.Copy).then_inc(acc_free[tt], 1)
            copy_tile(kT, 0)
            root()
            split_to(26)
            act.wait_ge(memory_set, 2)
            act.wait_ge(tr_copy, c.up("copy"))
            act.activation(kT2[0:64, 0, :], tb[0:64, 2, 0:T], ACT.Copy)
            act.activation(kT2[64:128, 1, :], tb[64:128, 2, 0:T], ACT.Copy).then_inc(tb_free[2], 1)
            split_to(30)
            copy_tile(kT, 4)
            split_to(32)
            copy_tile(qidxT, 0)
            split_to(34)
            copy_tile(qidxT, 4)
            split_to(36)
            copy_tile(qT, 0)
            split_to(38)
            copy_tile(qT, 4)
            for q in range(IH):
                split_to(40 + q)
                if 40 + q == 46:
                    tile_done()
                    read_out(lambda tt: v[:, tt, 0:N], 0)
                if 40 + q == 54:
                    tile_done()
                    read_out(lambda tt: v[:, tt, N:2 * N], 1)
                act.wait_ge(idx_ready, q + 1)
                if q >= 2:
                    act.wait_ge(relu_read, q - 1)
                w = P if q % 2 == 0 else T
                act.activation(rl[:, q % 2, 0:2 * w], tb[:, q % 2, 0:2 * w], ACT.Relu).then_inc(relu_ready, 1)
            for n in range(4):
                split_to(62 + 8 * n)
                tile_done()
                read_out(lambda tt: z[:, tt, n * N:(n + 1) * N], n % 2, ACT.Gelu_apprx_tanh)
                if n == 1:
                    root()
            with c.loop(act, HEADS1 // 2, unit=16, raw=24, att=4, copy=2) as turn:
                for e in range(2):
                    head = turn * 2 + e
                    act.activation(qs[:, e, :], qT[:, cols(head, 1), :].rearrange("p a t -> p (a t)"), ACT.Copy)\
                        .then_inc(copied, 1)
                    split(2)
                    for tt, at in ((0, slice(T, T + P)), (1, slice(0, T))):
                        act.wait_ge(att_ready, c.up("att"))
                        ins = act.activation(att1[:, at], att1[:, at], ACT.Exp, bias=nmax[:, tt:tt + 1],
                                             accum_out=esum[:, tt:tt + 1])
                    ins.then_inc(exp_ready, 1)
                    split(2)
                    act.wait_ge(tr_copy, c.up("copy"))
                    act.activation(pt1[:], tb[:, 1, 0:384], ACT.Copy).then_inc(tb_free[1], 1)
                    split(3)
                    tile_done(3)
                    read_out(lambda tt: sg[:, tt, cols(head * N, N)], e, ACT.Sigmoid)
                    split(1)
            take_hi_tile(Hh, 0)
            take_hi_tile(Hh, 4)
            act.dma_start(x[:], x_in).then_inc(x_loaded, 16)
            split(2)
            take_hi_tile(Hh, 8)
            split(2)
            take_hi_tile(Hh, 12)
            spread_rows(gm1)
            split(4)
            take_hi_tile(mergedh, 0)
            for j in range(1, 4):
                split(8)
                take_hi_tile(mergedh, j * 4)
            for t in range(4):
                split(7)
                square_tile(t % 2, t)
                if t < 3:
                    split(1)
            root()
            split(1)
            square_x()
            root()
            for k in range(KD // 2):
                act.wait_ge(tr_split, c.up("split"))
                for j in range(2):
                    ins = act.activation(Hh[:, 2 * k + j, :], tb[:, k % 4, j * T:(j + 1) * T], ACT.Identity,
                                         scale=fA[:, 2 * k + j:2 * k + j + 1],
                                         bias=modfm[:, SHIFT_F + 2 * k + j:SHIFT_F + 2 * k + j + 1])
                ins.then_inc(tr_hi, 1)
            def hidden(n):
                split(8)
                tile_done()
                read_out(lambda tt: sgt[:, tt, :], 0, ACT.Silu)
                split(8)
                take_hi_tile(hidh, n * 4)

            with c.loop(act, FFN_MOD, unit=16, raw=16 + MOD_UNITS, split=2) as n:
                hidden(n)
            with c.loop(act, FT - FFN_MOD, unit=16, raw=16, split=2) as n:
                hidden(n + FFN_MOD)
            spread_rows(gm2, (2, 3, 2, 3))
            for t in range(4):
                split(FK // 2 - 1)
                square_tile(t % 2, t)
                if t < 3:
                    split(1)
            root()
            split(1)
            act.wait_ge(x_ready, c.at("x") + 2 * TT)
            for k in range(KD // 2):
                act.wait_ge(tr_split, c.up("split"))
                take_hi(Hh, 2 * k, k % 4, lambda j: vec("norm_a", 2 * k + j))
            act.dma_start(poolM[:], pool_in).then_inc(pool_loaded, 16)
            act.dma_start(mask2[:], mask2_in).then_inc(mask_loaded, 16)
            square_x()
            root()
            act.wait_ge(rstd_ready, c.at("var"))
            with c.loop(act, 4, unit=20, raw=20, split=4) as g:
                split(8)
                tile_done()
                read_out(lambda tt: u[:, tt, :], 0, scaled=True)
                for b in range(2):
                    act.wait_ge(tr_split, c.up("split"))
                    take_hi(ph, 2 * b, 2 + b)
                split(4)
                split(4, N)
                tile_done()
                read_out(lambda tt: sgt[:, tt, :], 1, ACT.Silu, scaled=True)
                split(4)
                take_hi_tile(zh, g * 4, lambda j: vec("scale_a", g * 4 + j))
            c.n["acc0"] = c.n["acc1"] = TILES_BEFORE_OUT_A // 2
            with c.loop(act, 2, unit=16, raw=16, split=4, acc0=1, acc1=1) as i:
                for e in range(2):
                    split(8)
                    n = c.up(f"acc{e}")
                    for tt in range(TT):
                        act.wait_ge(acc_free[2 * e + tt], n + 1)
                        act.activation(x[:, tt, cols((i * 2 + e) * N, N)], tok[:, e, tt, :], ACT.Copy)
                        ins = act.activation(junk[:, tt, :], tok[:, e, tt, :], ACT.Square, accum_out=ssqp[:, tt, cols(i * 2 + e, 1)])
                    ins.then_inc(evac, 1)
                    for b in range(2):
                        act.wait_ge(tr_split, c.up("split"))
                        k = (i * 2 + e) * 4 + 2 * b
                        take_hi(Hh, k, b, lambda j: vec("norm_kv", k + j), last=False)
                        take_hi(hbh, k, b, lambda j: vec("norm_b", k + j))
            split(2)
            root()
            act.wait_ge(rstd_ready, c.at("var"))
            with c.loop(act, 4, unit=16, raw=16, copy=2) as i:
                split(6)
                copy_tile(k2T, i * 4)
                split(8)
                tile_done()
                read_out(lambda tt: v2[:, tt, cols(i * N, N)], 1, scaled=True)
                split(2)
            W = 2 * HN

            def attention(now=W, ahead=W):
                split(2, now)
                for b, k, nk in ((0, 0, 2), (1, 2, 1)):
                    act.wait_ge(tr_copy, c.up("copy"))
                    act.activation(qTh[:, k:k + nk, :], tb[:, b, 0:nk * T].rearrange("p (k t) -> p k t", k=nk), ACT.Copy)\
                        .then_inc(tb_free[b], 1)
                split(2, now)
                for tt, at in ((1, slice(0, NG * T)), (0, slice(NG * T, NG * (T + P)))):
                    act.wait_ge(att_ready, c.up("att"))
                    ins = act.activation(att2[:, at], att2[:, at], ACT.Exp, bias=nmax[:, tt:tt + 1],
                                         accum_out=esum[:, tt:tt + 1])
                ins.then_inc(exp_ready, 1)
                split(2, ahead)
                act.wait_ge(tr_copy, c.up("copy"))
                act.activation(pt2[:], tb[:, 3, 0:384], ACT.Copy).then_inc(tb_free[3], 1)
                split(2, ahead)

            split(6, W)
            with c.loop(act, HEADS2 // 2 - 1, unit=16, raw=16, copy=6, att=4):
                for e in range(2):
                    attention()
            attention(W, UNIT)
            for i in range(4):
                if i == 0:
                    attention(UNIT, UNIT)
                else:
                    split(8)
                tile_done()
                read_out(lambda tt: sgt[:, tt, :], i % 2, ACT.Silu, scaled=True)
                take_hi_tile(Hh, 4 * i)
            c.n["acc0"] = c.n["acc1"] = TILES_BEFORE_OUT_B // 2
            for i in range(4):
                split(8 if i < 3 else 4)
                n = c.up(f"acc{i % 2}")
                for tt in range(TT):
                    act.wait_ge(acc_free[2 * (i % 2) + tt], n + 1)
                    ins = act.activation(junk[:, tt, :], x[:, tt, i * N:(i + 1) * N], ACT.Square, accum_out=ssqp[:, tt, i:i + 1])
                ins.then_inc(evac, 1)
            root()

        @block.vector
        def _(dve):
            c = Counts()

            def chain(ins):
                ins.then_inc(dve_chain, 1)
                dve.wait_ge(dve_chain, c.up("chain"))

            def split(units, n=UNIT):
                for _ in range(units):
                    if c.n.get("unit", 0) in TAKES:
                        add_up_block()
                    if c.n.get("unit", 0) in LATE:
                        late_unit(LATE.index(c.n["unit"]))
                    r, s = c.slot("raw", RING), c.slot("unit", RING)
                    dve.wait_ge(hi_ready, c.up("unit"))
                    dve.tensor_tensor(lo[:, s, 0:n], raw[:, r, 0:n], hi[:, s, 0:n].bitcast(F32), ALU.subtract)\
                        .then_inc(unit_split, 1)
                    c.up("raw")

            def split_to(unit, n=UNIT):
                split(unit - c.n["unit"], n)

            def tile_done(ahead=RING):
                dve.wait_ge(unit_used, c.at("unit") + (RING - ahead))

            def late_unit(i):
                block, j = i // MOD_UNITS, i % MOD_UNITS
                dst = late_sums(block)
                if j == 0:
                    under_way = 0 if block in LOOPED else 1
                    dve.wait_ge(mod_read, c.at("late") + (START_BLOCKS + 2 - under_way))
                s = c.slot("raw", RING)
                dve.wait_ge(raw_loaded[s], c.at("raw", RING) * 16 + 16)
                for kk in range(2):
                    w, ck = raw[:, s, kk * N:(kk + 1) * N], vec("c", 2 * j + kk)
                    if j == kk == 0:
                        ins = dve.tensor_scalar(dst, w, ck, None, ALU.mult)
                    else:
                        ins = dve.scalar_tensor_tensor(dst, w, ck, dst, ALU.mult, ALU.add)
                    if kk == 0:
                        chain(ins)
                ins.then_inc(unit_split, 1)
                dve.wait_ge(unit_split, c.up("raw"))
                if j == MOD_UNITS - 1:
                    c.up("late")

            def add_up_block():
                dve.wait_ge(mod_read, c.at("took") + (START_BLOCKS + 2 + 1))
                dve.tensor_reduce(modfm[:, cols(c.at("took") * 4 + START_BLOCKS * 4, 4)],
                                  tb[:, 3, :].rearrange("p (q s) -> p q s", q=4), AX_X, ALU.add).then_inc(mod_taken, 1)
                c.up("took")

            def add_bias(start, n):
                dve.wait_ge(mod_taken, c.at("took") + QUARTERS)
                chain(dve.tensor_tensor(modfm[:, start:start + n], modfm[:, start:start + n], vec("b_mod", start, n), ALU.add))

            def gated_gain(gate, gain):
                dve.tensor_tensor(fG[:], modfm[:, gate:gate + KD], vec(gain, 0, KD), ALU.mult).then_inc(gate_ready, 1)

            def inverse_root():
                dve.wait_ge(std_ready, c.up("std"))
                dve.reciprocal(rstd[:], std[:]).then_inc(rstd_ready, 1)
                dve.wait_ge(rstd_ready, c.n["std"])

            def rms(n):
                dve.tensor_scalar(var[:], ssq[:], 1.0 / n, EPS, ALU.mult, ALU.add).then_inc(var_ready, 1)
                inverse_root()

            def sum_squares(parts=4):
                chain(dve.tensor_reduce(ssq[:], ssqp[:, :, 0:parts], AX_X, ALU.add))

            def layer_norm_stats(src, chunks):
                for tt in range(TT):
                    for i, chunk in enumerate(chunks):
                        ins = dve.bn_stats(stats[:, tt, i, :], src(tt, chunk))
                chain(ins)
                for tt in range(TT):
                    ins = dve.bn_aggr(mv[:, tt, :], stats[:, tt, 0:len(chunks), :])
                chain(ins)
                dve.tensor_scalar(var[:], mv[:, :, 1:2].rearrange("p t a -> p (t a)"), EPS, None, ALU.add)\
                    .then_inc(var_ready, 1)
                inverse_root()

            def rotate(pair, dst, heads, dim, half, cos, sin, width=N):
                h4 = lambda ap: ap.rearrange("p (h d) -> p h d", h=heads)
                spread = lambda ap: ap.unsqueeze(1).to_broadcast([P, heads, ap.shape[-1]])
                rot = 2 * half
                for tt in range(TT):
                    src, tmp, o = h4(acc[:, 2 * pair + tt, 0:width]), h4(sgt[:, tt, 0:width]), h4(dst(tt))
                    ins = dve.tensor_tensor(tmp[:, :, 0:half], src[:, :, half:rot], spread(sin[:, tt, 0:half]), ALU.mult)
                    if tt == 1:
                        chain(ins)
                    dve.tensor_tensor(tmp[:, :, half:rot], src[:, :, 0:half], spread(sin[:, tt, half:rot]), ALU.mult)
                    ins = dve.tensor_tensor(o[:, :, 0:rot], src[:, :, 0:rot], spread(cos[:, tt, 0:rot]), ALU.mult)
                    if rot < dim:
                        ins = dve.tensor_copy(o[:, :, rot:dim], src[:, :, rot:dim])
                    ins.then_inc(acc_free[2 * pair + tt], 1)
                for tt in range(TT):
                    tmp, o = h4(sgt[:, tt, 0:width]), h4(dst(tt))
                    ins = dve.tensor_tensor(o[:, :, 0:rot], o[:, :, 0:rot], tmp[:, :, 0:rot], ALU.add)
                    if tt == 0:
                        chain(ins)
                ins.then_inc(tok_ready, 1)

            def take_lo(dst, src_hi, k, b, gain=None, last=True):
                if gain is None:
                    ins = dve.tensor_tensor(dst[:, cols(k, 2), :], tb[:, b, :].rearrange("p (k t) -> p k t", k=2),
                                            src_hi[:, cols(k, 2), :].bitcast(F32), ALU.subtract)
                else:
                    for j in range(2):
                        ins = dve.scalar_tensor_tensor(dst[:, cols(k + j, 1), :], tb[:, b:b + 1, j * T:(j + 1) * T], gain(j),
                                                       src_hi[:, cols(k + j, 1), :].bitcast(F32), ALU.mult, ALU.subtract)
                if last:
                    ins.then_inc(tb_free[b], 1)

            def take_lo_tile(dst, src_hi, k, gain=None, banks=(0, 1)):
                for i, b in enumerate(banks):
                    dve.wait_ge(tr_hi, c.up("hi"))
                    take_lo(dst, src_hi, k + 2 * i, b, gain and (lambda j, i=i: gain(2 * i + j)))

            def masked_scores(att, parts, tokens):
                for dst, scores, mask, free in parts:
                    ins = dve.scalar_tensor_tensor(dst, scores, SCALE, mask, ALU.mult, ALU.add)
                    if free is not None:
                        ins.then_inc(free, 1)
                    else:
                        chain(ins)
                for i, (tt, at) in enumerate(tokens):
                    ins = dve.tensor_reduce(nmax[:, tt:tt + 1], att[:, at], AX_X, ALU.max, negate=True)
                    ins.then_inc(att_ready, 1)
                    dve.wait_ge(att_ready, c.up("att"))

            def start_block(b, quarter=None):
                dve.wait_ge(mod_read, c.up("block"))
                for j in range(MOD_UNITS):
                    s = c.slot("raw", RING)
                    dve.wait_ge(raw_loaded[s], c.at("raw", RING) * 16 + 16)
                    for kk in range(2):
                        dst, w, ck = macc0[:, b, kk, :], raw[:, s, kk * N:(kk + 1) * N], vec("c", 2 * j + kk)
                        if j == 0:
                            ins = dve.tensor_scalar(dst, w, ck, None, ALU.mult)
                        else:
                            dve.wait_ge(*((dve_chain, c.at("chain")) if kk == 0 else (unit_split, c.at("raw"))))
                            ins = dve.scalar_tensor_tensor(dst, w, ck, dst, ALU.mult, ALU.add)
                        if kk == 0:
                            ins.then_inc(dve_chain, 1)
                            c.up("chain")
                    ins.then_inc(unit_split, 1)
                    c.up("raw")
                    if quarter is not None and j == 2:
                        start_lo(quarter)

            def start_lo(q):
                k = q * 4
                dve.wait_ge(in_hi, c.up("in_hi"))
                dve.tensor_tensor(Hl[:, cols(k, 4), :], xnT[:, cols(k, 4), :], Hh[:, cols(k, 4), :].bitcast(F32), ALU.subtract)\
                    .then_inc(in_split, 1)

            def start_input(q, behind=1):
                dve.wait_ge(mod_read, c.at("block") + (2 - behind))
                m, k = q * 8, q * 4
                dve.tensor_tensor(modfm[:, cols(m, 8)], tb[:, 3, cols(m, 8)], vec("b_mod", m, 8), ALU.add)\
                    .then_inc(mod_taken, 1)
                dve.wait_ge(mod_taken, c.up("taken"))
                dve.scalar_tensor_tensor(fA[:, cols(k, 4)], modfm[:, cols(m, 4)], 1.0, vec("g_pre_mix", k, 4),
                                         ALU.add, ALU.mult).then_inc(fa_ready, 1)
                split(QUARTER_W)

            dve.wait_ge(fm_loaded, 16)
            start_block(0)
            start_block(1)
            dve.wait_ge(x_loaded, 16)
            dve.wait_ge(ssq_ready, c.up("ssq"))
            rms(D)
            for tt in range(TT):
                dve.tensor_scalar(xn[:, tt, :], x[:, tt, :], rstd[:, tt:tt + 1], None, ALU.mult).then_inc(xn_ready, 1)
            start_block(0)
            start_input(0)
            with c.loop(dve, QUARTERS - 2, raw=QUARTER, unit=QUARTER_W, block=2, taken=1, in_hi=1, chain=2 * MOD_UNITS) as q:
                start_block(1, q)
                start_block(0)
                start_input(q + 1)
            start_block(1, QUARTERS - 2)
            start_input(QUARTERS - 1, behind=0)
            start_lo(QUARTERS - 1)

            dve.wait_ge(const_in, 6 * 16)
            split_to(18, 640)
            dve.wait_ge(ssq_ready, c.up("ssq"))
            rms(QLAT)
            for tt in range(TT):
                dve.tensor_scalar(tok[:, 0, tt, :], acc[:, tt, :], rstd[:, tt:tt + 1], None, ALU.mult)\
                    .then_inc(acc_free[tt], 1)
            split_to(20)
            tile_done()
            rotate(1, lambda tt: tok[:, 1, tt, :], 4, HD, HD // 2, ropeC, ropeS)
            take_lo_tile(qlatl, qlath, 0, lambda j: vec("qlat_g", j))
            split_to(22)
            for tt in range(TT):
                dve.wait_ge(acc_free[tt], 3)
            layer_norm_stats(lambda tt, _: kx[:, tt, 0:IDIM], (0,))
            for tt in range(TT):
                ins = dve.tensor_scalar(kn[:, tt, :], kx[:, tt, 0:IDIM], mv[:, tt, 0:1], rstd[:, tt:tt + 1],
                                        ALU.subtract, ALU.mult)
            chain(ins)
            dve.wait_ge(row_loaded, 4 * 16)
            both = lambda i: kidx_gb[:, i:i + 1, :].to_broadcast([P, TT, IDIM])
            chain(dve.tensor_tensor(kn[:], kn[:], both(0), ALU.mult))
            chain(dve.tensor_tensor(kn[:], kn[:], both(1), ALU.add))
            ih = IROPE // 2
            dve.tensor_tensor(kr[:, :, 0:ih], kn[:, :, ih:IROPE], iropeS[:, :, 0:ih], ALU.mult)
            dve.tensor_tensor(kr[:, :, ih:IROPE], kn[:, :, 0:ih], iropeS[:, :, ih:IROPE], ALU.mult)
            dve.tensor_copy(kd[:, :, IROPE:IDIM], kn[:, :, IROPE:IDIM])
            chain(dve.tensor_tensor(kd[:, :, 0:IROPE], kn[:, :, 0:IROPE], iropeC[:], ALU.mult))
            chain(dve.tensor_tensor(kd[:, :, 0:IROPE], kd[:, :, 0:IROPE], kr[:], ALU.add))
            dve.tensor_scalar(kx[:, :, IDIM:], kx[:, :, IDIM:], IDX_SCALE, None, ALU.mult)
            dve.tensor_copy(kd[:, :, IDIM:], kd[:, :, 0:IDIM]).then_inc(kidx_ready, 1)
            split_to(29)
            tile_done(3)
            rotate(1, lambda tt: tok[:, 0, tt, :], 4, HD, HD // 2, ropeC, ropeS)
            for t in range(4):
                split_to(31 + 2 * t)
                tile_done(3)
                dve.wait_ge(tr_copy, K_COPIED + 2 * t)
                tile = lambda tt: tok[:, (t + 1) % 2, tt, :]
                if t < 2:
                    rotate(t % 2, tile, 8, IDIM, IROPE // 2, iropeC, iropeS)
                else:
                    rotate(t % 2, tile, 4, HD, HD // 2, ropeC, ropeS)
            keys = (slice(T, T + P), slice(0, T))

            for q in range(IH):
                split_to(40 + q)
                tt, h = q % 2, q - q % 2
                w = P if tt == 0 else T
                dve.wait_ge(relu_ready, q + 1)
                weight = lambda j: kx[:, tt, IDIM + h + j:IDIM + h + j + 1]
                if h == 0:
                    ins = dve.tensor_scalar(score[:, keys[tt]], rl[:, tt, 0:w], weight(0), None, ALU.mult)
                else:
                    ins = dve.scalar_tensor_tensor(score[:, keys[tt]], rl[:, tt, 0:w], weight(0), score[:, keys[tt]],
                                                   ALU.mult, ALU.add)
                chain(ins)
                dve.scalar_tensor_tensor(score[:, keys[tt]], rl[:, tt, w:2 * w], weight(1), score[:, keys[tt]],
                                         ALU.mult, ALU.add).then_inc(relu_read, 1)
            split_to(57)
            dve.wait_ge(relu_read, IH)
            diagonal = (slice(T, T + P), slice(P, T))
            for tt in range(TT):
                ins = dve.tensor_tensor(score[:, diagonal[tt]], score[:, diagonal[tt]], mask1[:], ALU.add)
            chain(ins)
            left = score
            for r in range(TOPK // 8):
                for tt in range(TT):
                    ins = dve.max(best8[:, tt, :], left[:, keys[tt]])
                chain(ins)
                for tt in range(TT):
                    ins = dve.match_replace(work[:, keys[tt]], best8[:, tt, :], left[:, keys[tt]], TAKEN)
                chain(ins)
                left = work
                split_to(58 + r)
            chain(dve.tensor_scalar(selb[:], work[:], TAKEN, -BIG, ALU.not_equal, ALU.mult))
            for tt in range(TT):
                ins = dve.tensor_tensor(selb[:, diagonal[tt]], selb[:, diagonal[tt]], mask1[:], ALU.add)
            split_to(70)
            for tt in range(TT):
                dve.wait_ge(acc_free[2 + tt], 11 // 2 + 2)
            layer_norm_stats(lambda tt, i: z[:, tt, i * N:(i + 1) * N], (0, 1))
            split_to(72)
            for tt in range(TT):
                ins = dve.tensor_scalar(z[:, tt, 0:GW], z[:, tt, 0:GW], mv[:, tt, 0:1], rstd[:, tt:tt + 1],
                                        ALU.subtract, ALU.mult)
            chain(ins)
            split_to(74)
            dve.wait_ge(row_loaded, 4 * 16)
            for row, op in ((ln_g, ALU.mult), (ln_b, ALU.add)):
                for tt in range(TT):
                    ins = dve.tensor_tensor(z[:, tt, 0:GW], z[:, tt, 0:GW], row[:], op)
                    if row is ln_g and tt == 1:
                        chain(ins)
                if row is ln_g:
                    split_to(76)
            ins.then_inc(v_normed, 1)

            def gate_u(first):
                for g in range(first, first + 4):
                    b = g // 2 % 2
                    if g % 2 == 0:
                        dve.wait_ge(gmlp_ready, c.up("gmlp"))
                    ug = z[:, :, GW + g * P:GW + (g + 1) * P]
                    ins = dve.scalar_tensor_tensor(ug, tb[:, b, (g % 2) * T:(g % 2 + 1) * T].rearrange("p (t d) -> p t d", t=TT),
                                                   vec("b_s", g), ug, ALU.add, ALU.mult)
                    if g % 2 == 1:
                        ins.then_inc(tb_free[b], 1)

            split_to(80)
            for tt in range(TT):
                dve.wait_ge(acc_free[tt], 12 // 2 + 2)
            gate_u(0)
            split_to(86)
            for tt in range(TT):
                dve.wait_ge(acc_free[2 + tt], 13 // 2 + 2)
            gate_u(4)
            with c.loop(dve, HEADS1 // 2, unit=16, raw=24, late=1, took=1, s=2, att=4, exp=2, o=2, chain=MOD_UNITS + 4) as turn:
                for e in range(2):
                    head = turn * 2 + e
                    split(2)
                    dve.wait_ge(s_ready, c.up("s"))
                    masked_scores(att1, [(att1[:, keys[tt]], tb[:, 0, keys[tt]], selb[:, keys[tt]], tb_free[0] if tt else None)
                                         for tt in range(TT)], [(tt, keys[tt]) for tt in range(TT)])
                    split(4)
                    dve.wait_ge(exp_ready, c.up("exp"))
                    chain(dve.reciprocal(resum[:], esum[:]))
                    dve.wait_ge(o_ready, c.up("o"))
                    for tt in range(TT):
                        ins = dve.tensor_scalar(O1[:, tt, cols(head * HD, HD)], tb[:, 2, tt * P:(tt + 1) * P],
                                                resum[:, tt:tt + 1], None, ALU.mult)
                    ins.then_inc(tb_free[2], 1)
                    split(2)
            take_lo_tile(Hl, Hh, 0)
            take_lo_tile(Hl, Hh, 4)
            split(2)
            take_lo_tile(Hl, Hh, 8)
            add_bias(GATE_M, KD)
            gated_gain(GATE_M, "g_post_mix")
            split(2)
            take_lo_tile(Hl, Hh, 12)

            def merge_a(j):
                tile_done()
                for tt in range(TT):
                    dve.tensor_tensor(tok[:, 0, tt, :], acc[:, tt, :], sg[:, tt, cols(j * N, N)], ALU.mult)\
                        .then_inc(acc_free[tt], 1)

            def merge_b(j):
                tile_done()
                for tt in range(TT):
                    dve.tensor_tensor(sgt[:, tt, :], acc[:, 2 + tt, :], sg[:, tt, cols(j * N + D, N)], ALU.mult)\
                        .then_inc(acc_free[2 + tt], 1)
                for tt in range(TT):
                    dve.wait_ge(acc_free[2 + tt], j + (TILES_BEFORE_MERGE // 2 + 2))
                    ins = dve.tensor_tensor(tok[:, 0, tt, :], tok[:, 0, tt, :], sgt[:, tt, :], ALU.add)
                ins.then_inc(tok_ready, 1)
                take_lo_tile(mergedl, mergedh, j * 4)

            merge_a(0)
            split(4)
            merge_b(0)
            for j in range(1, 4):
                split(4)
                merge_a(j)
                split(4)
                merge_b(j)

            def gated_tile(dst, gains, pair, col):
                for tt in range(TT):
                    dve.wait_ge(evac, c.up("evac"))
                    dve.tensor_tensor(dst[:, tt, cols(col, N)], acc[:, 2 * pair + tt, :], gains[:, cols(col, N)], ALU.mult)\
                        .then_inc(acc_free[2 * pair + tt], 1)

            def add_normed(src):
                sum_squares()
                rms(D)
                for n in (slice(0, D // 2), slice(D // 2, D)):
                    for tt in range(TT):
                        dve.scalar_tensor_tensor(x[:, tt, n], src[:, tt, n], rstd[:, tt:tt + 1], x[:, tt, n], ALU.mult, ALU.add)\
                            .then_inc(x_ready, 1)

            for t in range(4):
                split(7)
                if t == 3:
                    add_bias(SCALE_F, 2 * KD)
                    dve.scalar_tensor_tensor(fA[:], modfm[:, SCALE_F:SCALE_F + KD], 1.0, vec("g_pre_ffn", 0, KD), ALU.add, ALU.mult)
                gated_tile(mix, gm1, t % 2, t * N)
                if t < 3:
                    split(1)
            dve.wait_ge(x_loaded, 2 * 16)
            add_normed(mix)
            split(1)
            dve.wait_ge(ssq_ready, c.up("ssq"))
            sum_squares(2)
            rms(D)
            for n in (slice(0, D // 2), slice(D // 2, D)):
                for tt in range(TT):
                    dve.tensor_scalar(mix[:, tt, n], x[:, tt, n], rstd[:, tt:tt + 1], None, ALU.mult).then_inc(xn_ready, 1)
            for k in range(KD // 2):
                dve.wait_ge(tr_hi, c.up("hi"))
                for j in range(2):
                    kt = 2 * k + j
                    ins = dve.tensor_scalar(sgt[:, k % 2, j * T:(j + 1) * T], tb[:, k % 4, j * T:(j + 1) * T], fA[:, kt:kt + 1],
                                            modfm[:, SHIFT_F + kt:SHIFT_F + kt + 1], ALU.mult, ALU.add)
                chain(ins)
                dve.tensor_tensor(Hl[:, 2 * k:2 * k + 2, :], sgt[:, k % 2, :].rearrange("p (k t) -> p k t", k=2),
                                  Hh[:, 2 * k:2 * k + 2, :].bitcast(F32), ALU.subtract).then_inc(tb_free[k % 4], 1)

            def hidden(n):
                split(16)
                tile_done()
                for tt in range(TT):
                    dve.tensor_tensor(tok[:, 0, tt, :], acc[:, 2 + tt, :], sgt[:, tt, :], ALU.mult).then_inc(acc_free[2 + tt], 1)
                take_lo_tile(hidl, hidh, n * 4)

            hidden(0)
            with c.loop(dve, FFN_MOD - 1, unit=16, raw=16 + MOD_UNITS, hi=2, late=1, took=1, chain=MOD_UNITS) as n:
                hidden(n + 1)
            hidden(FFN_MOD)
            add_bias(GATE_F, KD)
            gated_gain(GATE_F, "g_post_ffn")
            with c.loop(dve, FT - FFN_MOD - 1, unit=16, raw=16, hi=2) as n:
                hidden(n + (FFN_MOD + 1))
            split(FK // 2 - 1)
            for t in range(4):
                gated_tile(fmix, gm2, t % 2, t * N)
                if t < 3:
                    split(FK // 2)
            add_normed(fmix)
            split(1)
            for k in range(KD // 2):
                dve.wait_ge(tr_hi, c.up("hi"))
                take_lo(Hl, Hh, 2 * k, k % 4, lambda j: vec("norm_a", 2 * k + j))
            dve.wait_ge(ssq_ready, c.up("ssq"))
            sum_squares(2)
            rms(D)
            with c.loop(dve, 4, unit=20, raw=20, hi=4) as g:
                split(8)
                take_lo_tile(pl, ph, 0, banks=(2, 3))
                split(4)
                split(4, N)
                split(4)
                tile_done()
                for tt in range(TT):
                    dve.tensor_tensor(tok[:, 1, tt, :], tb[:, 2 + tt, :], sgt[:, tt, :], ALU.mult).then_inc(tb_free[2 + tt], 1)
                take_lo_tile(zl, zh, g * 4, lambda j: vec("scale_a", g * 4 + j))
            with c.loop(dve, 2, unit=16, raw=16, hi=4) as i:
                for e in range(2):
                    split(8)
                    tile_done()
                    t = i * 2 + e
                    for tt in range(TT):
                        dve.tensor_tensor(tok[:, e, tt, :], acc[:, 2 * e + tt, :], x[:, tt, cols(t * N, N)], ALU.add)\
                            .then_inc(acc_free[2 * e + tt], 1)
                    for b in range(2):
                        k = t * 4 + 2 * b
                        dve.wait_ge(tr_hi, c.up("hi"))
                        take_lo(Hl, Hh, k, b, lambda j: vec("norm_kv", k + j), last=False)
                        take_lo(hbl, hbh, k, b, lambda j: vec("norm_b", k + j))
            split(2)
            dve.wait_ge(evac, c.up("evac", 4))
            sum_squares()
            rms(D)
            for table in (ropeC, ropeS):
                for tt in range(TT):
                    ins = dve.tensor_scalar(table[:, tt, :], table[:, tt, :], rstd[:, tt:tt + 1], None, ALU.mult)
            chain(ins)
            c.n["copy"] = COPIES_BEFORE_K2
            with c.loop(dve, 4, unit=16, raw=16, copy=2, chain=2):
                split(5)
                tile_done(3)
                dve.wait_ge(tr_copy, c.at("copy"))
                c.up("copy", 2)
                rotate(0, lambda tt: tok[:, 0, tt, :], 4, HD, HD // 2, ropeC, ropeS)
                split(11)
            dve.wait_ge(mask_loaded, 16)
            S1 = NG * T

            def turn_queries(pair):
                tile_done(3)
                rotate(pair, lambda tt: tok[:, 0, tt, 0:HN], NG, HD, HD // 2, ropeC, ropeS, HN)

            def attention(head, pair=None, now=2 * HN, ahead=2 * HN):
                split(4, now)
                dve.wait_ge(s_ready, c.up("s"))
                by_group = lambda ap: ap.rearrange("p (g t) -> p g t", t=P)
                masked_scores(att2, (
                    (att2[:, 0:2 * T], tb[:, 0, :], mask2[:, 0:2, :].rearrange("p g t -> p (g t)"), tb_free[0]),
                    (att2[:, 2 * T:S1], tb[:, 1, 0:T], mask2[:, 2, :], tb_free[1]),
                    (att2[:, S1:S1 + P], tb[:, 2, 0:P], mask2[:, 0, P:T], None),
                    (by_group(att2[:, S1 + P:]), by_group(tb[:, 2, P:NG * P]), mask2[:, 1:, P:T], tb_free[2])),
                    ((1, slice(0, S1)), (0, slice(S1, S1 + NG * P))))
                dve.wait_ge(exp_ready, c.up("exp"))
                dve.reciprocal(resum[:], esum[:])
                for g in range(1, NG):
                    for at, w in ((0, T), (S1, P)):
                        ins = dve.tensor_tensor(att2[:, at:at + w], att2[:, at:at + w], att2[:, at + g * w:at + (g + 1) * w],
                                                ALU.add)
                        if g == 1 and at:
                            chain(ins)
                ins.then_inc(p_ready, 1)
                split(3, ahead)
                if pair is not None:
                    turn_queries(pair)
                split(1, ahead)
                dve.wait_ge(o_ready, c.up("o"))
                for tt in range(TT):
                    ins = dve.tensor_scalar(O2[:, tt, cols(head * HD, HD)], tb[:, 2, tt * P:(tt + 1) * P], resum[:, tt:tt + 1],
                                            None, ALU.mult)
                ins.then_inc(tb_free[2], 1)

            split(5, 2 * HN)
            dve.wait_ge(tr_copy, c.at("copy"))
            turn_queries(0)
            split(1, 2 * HN)
            with c.loop(dve, HEADS2 // 2 - 1, unit=16, raw=16, s=2, att=4, exp=2, o=2, chain=8) as i:
                for e in range(2):
                    attention(i * 2 + e, 1 - e)
            attention(HEADS2 - 2, 1, ahead=UNIT)
            for i in range(4):
                if i == 0:
                    attention(HEADS2 - 1, now=UNIT, ahead=UNIT)
                else:
                    split(8)
                for tt in range(TT):
                    dve.wait_ge(acc_free[2 * (i % 2) + tt], (TILES_BEFORE_OUT_B - 4 + i) // 2 + 2)
                    ins = dve.tensor_tensor(tok[:, 0, tt, :], O2[:, tt, i * N:(i + 1) * N], sgt[:, tt, :], ALU.mult)
                ins.then_inc(tok_ready, 1)
                take_lo_tile(Hl, Hh, 4 * i)
            for i in range(4):
                split(8 if i < 3 else 4)
                tile_done(RING if i < 3 else 0)
                for tt in range(TT):
                    xt = x[:, tt, i * N:(i + 1) * N]
                    dve.tensor_tensor(xt, acc[:, 2 * (i % 2) + tt, :], xt, ALU.add).then_inc(acc_free[2 * (i % 2) + tt], 1)
            dve.wait_ge(evac, c.up("evac", 4))
            sum_squares()
            rms(D)
            dve.wait_ge(row_ready, 3 * 4)
            for tt in range(TT):
                for q in range(4):
                    xt = x[:, tt, q * N:(q + 1) * N]
                    dve.scalar_tensor_tensor(xt, xt, rstd[:, tt:tt + 1], tb[:, q, :], ALU.mult, ALU.mult).then_inc(out_ready, 1)

        @block.tensor
        def _(pe):
            c = Counts()
            pe.sem_inc(unit_used, RING)
            pe.sem_inc(mod_read, 2)
            for b in range(4):
                pe.sem_inc(acc_free[b], 1)
                pe.sem_inc(tb_free[b], 1)

            def products(dst, h, l, k, s, kts, n, first, last):
                for i in range(kts):
                    for tt in range(TT):
                        a, b = h[:, k + i, tt * P:(tt + 1) * P], l[:, k + i, tt * P:(tt + 1) * P]
                        w = slice(i * n, (i + 1) * n)
                        pe.matmul(dst(tt), a, hi[:, s, w], start=first and i == 0, stop=False)
                        pe.matmul(dst(tt), a, lo[:, s, w], start=False, stop=False)
                        mm = pe.matmul(dst(tt), b, hi[:, s, w], start=False, stop=last and i == kts - 1)
                mm.then_inc(unit_used, 1)

            def open_tile(pair, n=N):
                for tt in range(TT):
                    pe.wait_ge(acc_free[2 * pair + tt], c.at(f"acc{pair}") + 1)
                c.up(f"acc{pair}")
                return lambda tt: acc[:, 2 * pair + tt, 0:n]

            def unit(dst, h, l, k, kts, n, first, last):
                s = c.slot("unit", RING)
                c.up("raw", 1 + MODS.get(c.n.get("unit", 0), 0))
                c.up("unit")
                pe.wait_ge(unit_split, c.at("raw"))
                products(dst, h, l, k, s, kts, n, first, last)

            def tile(h, l, pair, units, n=N, kts=2, k=0, dst=None, before={}, after={}):
                if dst is None:
                    dst = open_tile(pair, n)
                for i in range(units):
                    if i in before:
                        before[i]()
                    unit(dst, h, l, k + kts * i, kts, n, i == 0, i == units - 1)
                    if i in after:
                        after[i]()

            def read_out(pair):
                for tt in range(TT):
                    pe.wait_ge(acc_free[2 * pair + tt], c.at(f"acc{pair}") + 1)

            def taken(*banks):
                for b in banks:
                    pe.wait_ge(tb_free[b], c.at(f"tb{b}") + 1)

            def fill(b):
                taken(b)
                c.up(f"tb{b}")

            def transpose_pair(src, b, done):
                fill(b)
                for j in range(2):
                    for tt in range(TT):
                        ins = pe.transpose(tb[:, b, j * T + tt * P:j * T + (tt + 1) * P], src(tt, j), ident[:])
                ins.then_inc(done, 1)

            def transpose_tile(src, done):
                for b in range(2):
                    transpose_pair(lambda tt, j: src(tt)[:, (2 * b + j) * P:(2 * b + j + 1) * P], b, done)

            def transpose_tok(slot, done):
                transpose_tile(lambda tt: tok[:, slot, tt, :], done)

            def turned(slot, done=tr_copy):
                pe.wait_ge(tok_ready, c.up("tok"))
                transpose_tok(slot, done)

            def mod_sum(block, parts):
                for q in range(4):
                    for i, part in enumerate(parts):
                        ins = pe.matmul(tb[:, 3, cols(block * 4 + q, 1)], part[:, q * P:(q + 1) * P], ones[:],
                                        start=i == 0, stop=i == len(parts) - 1)
                ins.then_inc(mod_read, 1)

            def late_sum(block):
                pe.wait_ge(mod_taken, c.at("late") + QUARTERS)
                for q in range(4):
                    ins = pe.transpose(tb[:, 3, q * P:(q + 1) * P], late_sums(block)[:, q * P:(q + 1) * P], ident[:])
                ins.then_inc(mod_read, 1)
                c.up("late")

            def spread(src, bank):
                for q in range(4):
                    b = bank(q)
                    fill(b)
                    for j in range(4):
                        ins = pe.matmul(tb[:, b, j * P:(j + 1) * P], src(4 * q + j).to_broadcast([P, P]), ident[:],
                                        start=True, stop=True)
                    ins.then_inc(row_ready, 1)

            pe.wait_ge(const_in, 6 * 16)
            pe.wait_ge(memory_set, 1)
            latent, keys = open_tile(0), open_tile(1)

            def start_sum(block):
                pe.wait_ge(unit_split, units_to_block(block))
                mod_sum(block, [macc0[:, block % 2, kk, :] for kk in range(2)])

            start_sum(0)
            start_sum(1)
            pe.wait_ge(xn_ready, TT)
            for k in range(KD // 2):
                transpose_pair(lambda tt, j: xn[:, tt, (2 * k + j) * P:(2 * k + j + 1) * P], k % 3, tr_copy)
            for q in range(QUARTERS):
                if q < QUARTERS - 1:
                    pe.wait_ge(mod_taken, q + 1)
                    start_sum(2 * q + 2)
                pe.wait_ge(in_split, q + 1)
                for dst in (latent, keys):
                    for i in (0, 1):
                        unit(dst, Hh, Hl, 4 * q + 2 * i, 2, N, q == i == 0, q == QUARTERS - 1 and i == 1)
                if q < QUARTERS - 1:
                    start_sum(2 * q + 3)
            tile(Hh, Hl, 0, 2, n=80, kts=8)

            def latent_turned():
                transpose_tok(0, tr_split)

            latent_turned()

            def index_keys():
                pe.wait_ge(kidx_ready, 1)
                fill(2)
                for tt in range(TT):
                    ins = pe.transpose(tb[:, 2, tt * P:(tt + 1) * P], kd[:, tt, :], ident[:])
                ins.then_inc(tr_copy, 1)

            tile(Hh, Hl, 1, 8, after={1: lambda: turned(1), 5: index_keys})
            for t in range(4):
                tile(qlath, qlatl, t % 2, 2, after={1: lambda: turned(t % 2)})

            def logits(q):
                if q == 0:
                    taken(0, 1, 2)
                if q >= 2:
                    pe.wait_ge(relu_ready, q - 1)
                b, w = q % 2, P if q % 2 == 0 else T
                pe.matmul(tb[:, b, 0:2 * w].rearrange("p (h s) -> p h s", h=2), qidxT[:, q // 2, b * P:(b + 1) * P],
                          kT2[:, :, 0:w], start=True, stop=True).then_inc(idx_ready, 1)

            def after_values(first, units=8):
                return {i: (lambda q=first + i: logits(q)) for i in range(units) if 0 <= first + i < IH}

            hooks = after_values(-2)
            hooks[1] = lambda: turned(0)
            tile(Hh, Hl, 0, 8, after=hooks)
            tile(Hh, Hl, 1, 8, after=after_values(6))
            hooks = after_values(14)
            hooks[7] = lambda: late_sum(0)
            tile(Hh, Hl, 0, 8, after=hooks)
            tile(Hh, Hl, 1, 8)

            def spatial(first):
                if first == 0:
                    pe.wait_ge(v_normed, 1)
                    pe.wait_ge(ws_ready, 1)
                    pe.wait_ge(relu_ready, IH)
                for g in range(first, first + 4):
                    b = g // 2 % 2
                    if g % 2 == 0:
                        fill(b)
                    ins = pe.matmul(tb[:, b, (g % 2) * T:(g % 2 + 1) * T].rearrange("p (t d) -> p t d", t=TT), wsT[:, g, :],
                                    z[:, :, g * P:(g + 1) * P], start=True, stop=True)
                    if g % 2 == 1:
                        ins.then_inc(gmlp_ready, 1)

            tile(Hh, Hl, 0, 8, after={3: lambda: late_sum(1)})
            tile(Hh, Hl, 1, 8, after={3: lambda: spatial(0), 7: lambda: spatial(4)})
            with c.loop(pe, HEADS1 // 2, unit=16, raw=24, acc0=1, acc1=1, tb0=2, tb1=2, tb2=2, late=1, head=2, exp=2):
                for e in range(2):
                    head = c.at("head")

                    def scores():
                        pe.wait_ge(copied, c.up("head"))
                        fill(0)
                        pe.matmul(tb[:, 0, 0:T], qs[:, e, P:T], kT[:, cols(head, 1), :].rearrange("p a t -> p (a t)"),
                                  start=True, stop=True)
                        pe.matmul(tb[:, 0, T:T + P], qs[:, e, 0:P], kT[:, cols(head, 1), 0:P].rearrange("p a t -> p (a t)"),
                                  start=True, stop=True).then_inc(s_ready, 1)

                    def key_major():
                        pe.wait_ge(exp_ready, c.up("exp"))
                        fill(1)
                        for i in range(3):
                            ins = pe.transpose(tb[:, 1, i * P:(i + 1) * P], att1[:, i * P:(i + 1) * P], ident[:])
                        ins.then_inc(tr_copy, 1)

                    def output():
                        taken(1)
                        fill(2)
                        vh = lambda tt: v[:, tt, cols(head * HD, HD)]
                        pe.matmul(tb[:, 2, 0:HD], pt1[:, T:T + P], vh(0), start=True, stop=True)
                        pe.matmul(tb[:, 2, HD:2 * HD], pt1[:, 0:P], vh(0), start=True, stop=False)
                        pe.matmul(tb[:, 2, HD:2 * HD], pt1[:, P:T], vh(1), start=False, stop=True).then_inc(o_ready, 1)

                    hooks = {1: scores, 4: key_major, 6: output}
                    if e == 0:
                        hooks[2] = lambda: late_sum(LOOPED[0] - 1)
                    tile(Hh, Hl, e, 8, after=hooks)
            taken(0, 1)
            split_y = {}
            for k in range(4):
                transpose_pair(lambda tt, j: z[:, tt, GW + (2 * k + j) * P:GW + (2 * k + j + 1) * P], k % 2, tr_split)
                split_y[k] = lambda b=k % 2, n=c.at(f"tb{k % 2}") + 1: pe.wait_ge(tb_free[b], n)

            def attended(g):
                taken(2)
                transpose_tile(lambda tt: O1[:, tt, g * N:(g + 1) * N], tr_split)

            def spread_gate_m():
                pe.wait_ge(gate_ready, 1)
                spread(lambda j: fG[:, j:j + 1], lambda q: 2)

            def second_attended():
                attended(1)
                spread_gate_m()

            split_now = lambda: taken(0, 1)
            def first_attended():
                late_sum(LOOPED[3])
                attended(0)

            tile(Hh, Hl, 0, 4, before=split_y, after={1: first_attended, 3: second_attended})
            tile(Hh, Hl, 1, 4, k=8, before={0: split_now})
            for j in range(1, 4):
                hooks = {1: lambda: turned(0, tr_split)}
                tile(Hh, Hl, 0, 4, after=hooks)
                tile(Hh, Hl, 1, 4, k=8, after={3: lambda: late_sum(7)} if j == 2 else {})
            for t in range(4):
                hooks = {4: lambda: late_sum(8 + t)}
                if t == 0:
                    hooks[1] = lambda: turned(0, tr_split)
                tile(mergedh, mergedl, t % 2, 8, before={6: split_now} if t == 0 else {}, after=hooks)
            pe.wait_ge(mod_taken, c.at("late") + QUARTERS)
            split_by = []
            for k in range(KD // 2):
                if k % 4 == 0:
                    pe.wait_ge(xn_ready, TT + TT * (k // 4 + 1))
                transpose_pair(lambda tt, j: mix[:, tt, (2 * k + j) * P:(2 * k + j + 1) * P], k % 4, tr_split)
                split_by.append((tb_free[k % 4], c.at(f"tb{k % 4}") + 1))

            def when_split(units):
                return {j: (lambda j=j: pe.wait_ge(*units[j])) for j in range(8)}

            def next_hidden(after={}):
                def hidden():
                    read_out(1)
                    transpose_tok(0, tr_split)

                tile(Hh, Hl, 0, 8, after={1: hidden, **after})
                tile(Hh, Hl, 1, 8)

            tile(Hh, Hl, 0, 8, before=when_split(split_by))
            tile(Hh, Hl, 1, 8)
            def gate_f_sum():
                taken(3)
                late_sum(LOOPED[-1])

            with c.loop(pe, FFN_MOD - 1, unit=16, raw=16 + MOD_UNITS, acc0=1, acc1=1, tb0=1, tb1=1, late=1):
                next_hidden({3: gate_f_sum})
            next_hidden({3: gate_f_sum})
            with c.loop(pe, FT - FFN_MOD - 1, unit=16, raw=16, acc0=1, acc1=1, tb0=1, tb1=1):
                next_hidden()

            def last_hidden():
                read_out(1)
                transpose_tok(0, tr_split)
                pe.wait_ge(gate_ready, 2)
                spread(lambda j: fG[:, j:j + 1], lambda q: 2 + q % 2)

            for t in range(4):
                if t == 0:
                    tile(hidh, hidl, 0, FK // 2, before={FK // 2 - 2: split_now}, after={1: last_hidden})
                else:
                    tile(hidh, hidl, t % 2, FK // 2)
            pe.wait_ge(mod_taken, c.at("late") + QUARTERS)
            split_by = []
            for k in range(KD // 2):
                if k % 4 == 0:
                    pe.wait_ge(x_ready, 2 * TT + TT * (k // 4 + 1))
                transpose_pair(lambda tt, j: x[:, tt, (2 * k + j) * P:(2 * k + j + 1) * P], k % 4, tr_split)
                split_by.append((tb_free[k % 4], c.at(f"tb{k % 4}") + 1))
            def pooling_group(g, before={}, after={}):
                def pooled():
                    pe.wait_ge(pool_loaded, 16)
                    read_out(0)
                    for b in range(2):
                        fill(2 + b)
                        for j in range(2):
                            us = lambda s: u[:, s, (2 * b + j) * P:(2 * b + j + 1) * P]
                            m = lambda at, n: poolM[:, cols(g, 1), at:at + n].rearrange("p a t -> p (a t)")
                            at = j * T
                            pe.matmul(tb[:, 2 + b, at:at + T], us(0), m(0, T), start=True, stop=False)
                            ins = pe.matmul(tb[:, 2 + b, at + P:at + T], us(1), m(T, P), start=False, stop=True)
                        ins.then_inc(tr_split, 1)

                def group_banks():
                    fill(2)
                    fill(3)

                tile(Hh, Hl, 0, 8, before=before, after=after)
                tile(Hh, Hl, 1, 8, after={1: pooled})
                tile(ph, pl, None, 4, kts=1, dst=lambda tt: tb[:, 2 + tt, :], before={0: group_banks})

            def last_group():
                taken(2, 3)
                transpose_tok(1, tr_split)

            pooling_group(0, before=when_split(split_by))
            with c.loop(pe, 3, unit=20, raw=20, acc0=1, acc1=1, tb0=1, tb1=1, tb2=2, tb3=2) as g:
                pooling_group(g + 1, after={1: last_group})
            with c.loop(pe, 2, unit=16, raw=16, acc0=1, acc1=1, tb0=2, tb1=2):
                for e in range(2):
                    def last_tile():
                        taken(2, 3)
                        read_out(1 - e)
                        transpose_tok(1 - e, tr_split)

                    tile(zh, zl, e, 8, before={6: split_now}, after={1: last_tile})
            def last_out():
                read_out(1)
                transpose_tok(1, tr_split)

            tile(Hh, Hl, 0, 8, before={6: split_now}, after={1: last_out})
            tile(Hh, Hl, 1, 8, after={1: lambda: turned(0)})
            with c.loop(pe, 3, unit=16, raw=16, acc0=1, acc1=1, tb0=1, tb1=1, tok=1):
                tile(Hh, Hl, 0, 8)
                tile(Hh, Hl, 1, 8, after={1: lambda: turned(0)})

            def attention(head):
                def turned_queries():
                    pe.wait_ge(tok_ready, c.up("tok"))
                    for b, gs in ((0, (0, 1)), (1, (2,))):
                        fill(b)
                        for g in gs:
                            for tt in range(TT):
                                ins = pe.transpose(tb[:, b, (g % 2) * T + tt * P:(g % 2) * T + (tt + 1) * P],
                                                   tok[:, 0, tt, g * P:(g + 1) * P], ident[:])
                        ins.then_inc(tr_copy, 1)

                def scores():
                    k = lambda n: k2T[:, cols(head, 1), 0:n].rearrange("p a t -> p (a t)")
                    fill(0)
                    fill(1)
                    for g in range(NG):
                        pe.matmul(tb[:, g // 2, (g % 2) * T:(g % 2 + 1) * T], qTh[:, g, P:T], k(T), start=True, stop=True)
                    fill(2)
                    for g in range(NG):
                        ins = pe.matmul(tb[:, 2, g * P:(g + 1) * P], qTh[:, g, 0:P], k(P), start=True, stop=True)
                    ins.then_inc(s_ready, 1)

                def key_major():
                    pe.wait_ge(p_ready, c.up("p"))
                    fill(3)
                    S1 = NG * T
                    for i, at in enumerate((0, P, S1)):
                        ins = pe.transpose(tb[:, 3, i * P:(i + 1) * P], att2[:, at:at + P], ident[:])
                    ins.then_inc(tr_copy, 1)

                def output():
                    taken(3)
                    fill(2)
                    vh = lambda tt: v2[:, tt, cols(head * HD, HD)]
                    pe.matmul(tb[:, 2, 0:HD], pt2[:, T:T + P], vh(0), start=True, stop=True)
                    pe.matmul(tb[:, 2, HD:2 * HD], pt2[:, 0:P], vh(0), start=True, stop=False)
                    pe.matmul(tb[:, 2, HD:2 * HD], pt2[:, P:T], vh(1), start=False, stop=True).then_inc(o_ready, 1)

                return {1: turned_queries, 3: scores, 6: key_major, 7: output}

            tile(hbh, hbl, 0, 8, n=HN)
            with c.loop(pe, HEADS2 // 2 - 1, unit=16, raw=16, acc0=1, acc1=1, tb0=4, tb1=4, tb2=4, tb3=2, tok=2, p=2) as i:
                for e in range(2):
                    tile(hbh, hbl, 1 - e, 8, n=HN, after=attention(i * 2 + e))
            tile(hbh, hbl, 1, 8, n=HN, after=attention(HEADS2 - 2))
            tile(hbh, hbl, 0, 8, after=attention(HEADS2 - 1))
            for t in range(1, 4):
                tile(hbh, hbl, t % 2, 8, after={1: lambda: turned(0, tr_split)})
            for t in range(4):
                if t == 0:
                    tile(Hh, Hl, 0, 8, before={6: split_now}, after={1: lambda: turned(0, tr_split)})
                else:
                    tile(Hh, Hl, t % 2, 8)
            spread(lambda j: vec("norm_f", j), lambda q: q)


def _units(w, kts=2):
    k, n = w.shape
    return w.reshape(k // (kts * P), kts, P, n // N, N).transpose(3, 0, 2, 1, 4).reshape(-1, P, kts * N)


def _fm(v):
    return v.reshape(-1, P).T


def _rope(dim):
    inv = 1.0 / (np.float32(10000.0) ** (np.arange(0, dim, 2, dtype=np.float32) / np.float32(dim)))
    ang = np.arange(T, dtype=np.float32)[:, None] * inv[None, :].astype(np.float32)
    cos, sin = np.cos(ang), np.sin(ang)
    lay = lambda a: a.reshape(TT, P, dim).transpose(1, 0, 2).reshape(P, TT * dim)
    return lay(np.concatenate([cos, cos], 1)), lay(np.concatenate([-sin, sin], 1))


def _constants():
    table = np.concatenate([np.eye(P), *_rope(HD), *_rope(IROPE)], 1).astype(np.float32)
    t, s = np.arange(T)[:, None], np.arange(T)[None, :]
    mask1 = np.where(s <= t, 0, -BIG)[:P, :P].astype(np.float32)
    mask2 = np.stack([np.where((s <= t) & (t - s <= window) & ((t - s) % d == 0), 0, -BIG)[P:]
                      for window, d in ((128, 1), (512, 4), (2048, 16))], 1).astype(np.float32)
    pool = []
    for window in (2, 4, 8, 16):
        m = np.where((s <= t) & (s > t - window), 1.0 / np.minimum(t + 1, window), 0.0) - np.eye(T)
        pool.append(np.concatenate([m.T[:P], m.T[P:, P:]], 1))
    return table, mask1, mask2, np.stack(pool, 1).astype(np.float32)


def _layout(a):
    w_mod, b_mod = a["w_mod"][0], a["b_mod"][0]
    w_in, w_in_a, w_in_b = a["w_in"][0], a["w_in_a_2"][0], a["w_in_b_2"][0]
    shift_m, scale_m, gate_m, shift_f, scale_f, gate_f = range(6)
    blocks = [m * D + b * N for b in range(4) for m in (scale_m, shift_m)]
    blocks += [m * D + b * N for m in (gate_m, scale_f, shift_f, gate_f) for b in range(4)]
    wmod = [_units(w_mod[:, at:at + N]) for at in blocks]
    b_mod = np.concatenate([b_mod[at:at + N] for at in blocks])

    fm = np.concatenate([_fm(v) for v in (
        a["c"][0], b_mod, a["g_pre_mix"][0], a["g_post_mix"][0], a["q_lat_norm_g"][0], a["g_pre_ffn"][0],
        a["g_post_ffn"][0], a["norm_a_2"][0], a["scale_a_2"][0], a["norm_kv_2"], a["norm_b_2"][0], a["norm_f_2"],
        a["gmlp_b_s"][0].reshape(-1))], 1)
    assert fm.shape == (P, FM_COLS)

    at_q, at_k = 2 * GW, 2 * GW + QLAT
    at_v = at_k + GW
    at_i = at_v + GW
    at_g = at_i + IDIM + IH
    kidx = np.zeros((2, P, UNIT), np.float32)
    kidx[:, :, 0:640] = w_in[:, at_i:at_g].reshape(2, 8, P, 80).transpose(0, 2, 1, 3).reshape(2, P, 640)
    latent, keys = _units(w_in[:, at_q:at_k]), _units(w_in[:, at_k:at_k + N])
    wa = [w[2 * q:2 * q + 2] for q in range(QUARTERS) for w in (latent, keys)]
    wa += [kidx, _units(w_in[:, at_k + N:at_v]), _units(a["w_qidx_up"][0]), _units(a["w_q_up"][0]),
          _units(w_in[:, at_v:at_i]), _units(w_in[:, GW:at_q]), _units(w_in[:, 0:GW]), _units(w_in[:, at_g:])]

    def by_tile(*ws):
        return [_units(w[:, n:n + N]) for n in range(0, ws[0].shape[1], N) for w in ws]

    wa += by_tile(a["w_proj_a"][0], a["w_proj_b"][0])
    wa += [_units(a["w_out"][0])]
    wa += by_tile(a["w_ffn_gate"][0], a["w_ffn_up"][0])
    wa += [_units(a["w_ffn_down"][0])]
    for g in range(4):
        grp = np.zeros((4, P, UNIT), np.float32)
        grp[:, :, 0:N] = a["w_grp_a_2"][0, g].reshape(4, P, N)
        wa += [_units(w_in_a[:, g * N:(g + 1) * N]), _units(w_in_a[:, D + g * N:D + (g + 1) * N]), grp]
    wa += [_units(a["w_out_a_2"][0])]
    wa += by_tile(a["w_k_2"], a["w_v_2"])
    wq = w_in_b[:, 0:NG * D].reshape(KD // 2, 2, P, NG, HEADS2, HD).transpose(4, 0, 2, 1, 3, 5)
    wc = [_units(w_in_b[:, NG * D:]), _units(a["w_out_b_2"][0])]

    wa, wmod, stream, at = np.concatenate(wa), np.concatenate(wmod), [], 0
    assert wa.shape[0] == A_UNITS
    marks = sorted(MODS)
    for first, end in zip(marks, marks[1:] + [A_UNITS]):
        stream += [wmod[at:at + MODS[first]], wa[first:end]]
        at += MODS[first]
    stream = np.concatenate(stream)

    table, mask1, mask2, pool = _constants()
    kidx_gb = np.broadcast_to(np.stack([a["kidx_ln_g"][0], a["kidx_ln_b"][0]]), (P, 2, IDIM))
    arrays = [a["x"][0].reshape(TT, P, D).transpose(1, 0, 2), fm, np.stack([a["gmlp_ln_g"][0], a["gmlp_ln_b"][0]]), table,
              mask1, mask2, pool, a["gmlp_w_s"][0].transpose(2, 0, 1), kidx_gb,
              stream, wq.reshape(B_UNITS, P, 2 * HN), np.concatenate(wc)]
    assert arrays[-3].shape[0] == STREAM and arrays[-1].shape[0] == C_UNITS
    return [np.ascontiguousarray(v) for v in arrays]


_INS = ["x", "fm", "row", "table", "mask1", "mask2", "pool", "ws", "kidx", "wa", "wb", "wc"]


def kernel(**inputs):
    import concourse.bacc as bacc
    from concourse.bass_utils import run_bass_kernel_spmd

    nc = bacc.Bacc("TRN2", target_bir_lowering=False, num_devices=1)
    arrays, args = {}, []
    for name, v in zip(_INS, _layout({k: np.asarray(v) for k, v in inputs.items()})):
        arrays[f"in_{name}_dram"] = v
        args.append(nc.dram_tensor(f"in_{name}_dram", v.shape, mybir.dt.from_np(v.dtype), kind="ExternalInput").ap())
    out = nc.dram_tensor("out_0_dram", (1, T, D), F32, kind="ExternalOutput").ap()
    two_blocks(nc, *args, out[0])
    r = run_bass_kernel_spmd(nc, [arrays], core_ids=[0])
    return r.results[0]["out_0_dram"]
```
